# Optimizing a Trainium2 kernel written in Bass

```python
import jax, jax.numpy as jnp
from jax import lax
import numpy as np
import jax
import jax.numpy as jnp

D_MODEL = 1024
BATCH = 1
SEQ = 512
DEPTH = 1

HG_HEADS = 8
HG_HEAD_DIM = 128
HG_WIDTH = HG_HEADS * HG_HEAD_DIM
HG_CHUNK = 64
LRU_WIDTH = D_MODEL
LRU_HEADS = 8
LRU_HEAD_DIM = LRU_WIDTH // LRU_HEADS
LRU_CONV = 4
LRU_C = 8.0
CONV_WIDTH = D_MODEL
CONV_KERNEL = 31
N_BRANCH = 3
D_FF = 2816
MIX_COLS = (4 * HG_WIDTH) + (2 * LRU_WIDTH) + (2 * CONV_WIDTH) + (N_BRANCH * D_MODEL)


def rmsnorm(x, g, eps=1e-6):
    xf = x.astype(jnp.float32)
    y = xf * lax.rsqrt(jnp.mean(xf * xf, axis=-1, keepdims=True) + eps)
    return (y * g.astype(jnp.float32)).astype(x.dtype)

def layernorm(x, g, b, eps=1e-5):
    xf = x.astype(jnp.float32)
    mu = jnp.mean(xf, axis=-1, keepdims=True)
    xc = xf - mu
    y = xc * lax.rsqrt(jnp.mean(xc * xc, axis=-1, keepdims=True) + eps)
    return (y * g.astype(jnp.float32) + b.astype(jnp.float32)).astype(x.dtype)

def swiglu_ffn(x, w_in, w_out):
    g, u = jnp.split(x @ w_in, 2, axis=-1)
    return (jax.nn.silu(g) * u) @ w_out

def causal_dwconv(x, w, b):
    k = w.shape[0]
    xp = jnp.pad(x, ((0, 0), (k - 1, 0), (0, 0)))
    y = lax.conv_general_dilated(
        xp, w[:, None, :].astype(x.dtype), window_strides=(1,), padding='VALID',
        dimension_numbers=('NWC', 'WIO', 'NWC'), feature_group_count=x.shape[-1])
    return y + b

def hgrn2_chunked(q, k, v, log_f):
    b_, s_, h_, dk = q.shape
    dv = v.shape[-1]
    n = s_ // HG_CHUNK

    def to_chunks(t):
        return t.reshape(b_, n, HG_CHUNK, h_, t.shape[-1]).transpose(1, 0, 3, 2, 4)

    qc, kc, vc, gc = to_chunks(q), to_chunks(k), to_chunks(v), to_chunks(log_f)
    causal = jnp.tril(jnp.ones((HG_CHUNK, HG_CHUNK), dtype=bool))[:, :, None]

    def step(state, inp):
        qb, kb, vb, gb = inp
        bcum = jnp.cumsum(gb, axis=2)
        diff = bcum[:, :, :, None, :] - bcum[:, :, None, :, :]
        decay = jnp.exp(jnp.where(causal, diff, -jnp.inf))
        scores = jnp.einsum('bhtk,bhsk,bhtsk->bhts', qb, kb, decay)
        o = (jnp.einsum('bhts,bhsv->bhtv', scores, vb)
             + jnp.einsum('bhtk,bhkv->bhtv', qb * jnp.exp(bcum), state))
        b_last = bcum[:, :, -1:, :]
        state = (jnp.exp(b_last[:, :, 0, :])[..., None] * state
                 + jnp.einsum('bhsk,bhsv->bhkv', kb * jnp.exp(b_last - bcum), vb))
        return state, o

    s0 = jnp.zeros((b_, h_, dk, dv), jnp.float32)
    _, o = lax.scan(step, s0, (qc, kc, vc, gc))
    return o.transpose(1, 0, 3, 2, 4).reshape(b_, s_, h_, dv)

def linear_scan(a, u):
    def combine(c1, c2):
        a1, b1 = c1
        a2, b2 = c2
        return a1 * a2, a2 * b1 + b2
    _, h = lax.associative_scan(combine, (a, u), axis=1)
    return h

def hybrid_mixer(u, lb, w_in, b_in, hg_norm, lru_conv_w, lru_conv_b, lru_gate_w, lru_gate_b,
                 lru_lambda, cv_dw_w, cv_dw_b, cv_ln_g, cv_ln_b, w_branch, w_out):
    bsz, s_, _ = u.shape
    f32 = jnp.float32
    proj = u @ w_in + b_in
    sizes = [HG_WIDTH] * 4 + [LRU_WIDTH] * 2 + [CONV_WIDTH] * 2 + [D_MODEL] * N_BRANCH
    cuts = [int(c) for c in np.cumsum(sizes)[:-1]]
    hq, hf, hi, hg, lx, lg, ca, cb, g_a, g_b, g_c = jnp.split(proj, cuts, axis=-1)

    hshape = (bsz, s_, HG_HEADS, HG_HEAD_DIM)
    q = jax.nn.silu(hq.astype(f32)).reshape(hshape)
    z = hf.astype(f32).reshape(hshape)
    lb_h = lb.astype(f32).reshape(HG_HEADS, HG_HEAD_DIM)
    f = lb_h + (1.0 - lb_h) * jax.nn.sigmoid(z)
    k = (1.0 - lb_h) * jax.nn.sigmoid(-z)
    v = hi.astype(f32).reshape(hshape)
    o_hg = hgrn2_chunked(q, k, v, jnp.log(f))
    y_hg = rmsnorm(o_hg, hg_norm).reshape(bsz, s_, HG_WIDTH).astype(u.dtype) * jax.nn.silu(hg)

    xb = causal_dwconv(lx, lru_conv_w, lru_conv_b)
    xh = xb.reshape(bsz, s_, LRU_HEADS, LRU_HEAD_DIM)
    gates = jnp.einsum('bshi,ghij->gbshj', xh, lru_gate_w).reshape(2, bsz, s_, LRU_WIDTH)
    gates = gates.astype(f32) + lru_gate_b.astype(f32)[:, None, None, :]
    r_t = jax.nn.sigmoid(gates[0])
    i_t = jax.nn.sigmoid(gates[1])
    log_a = -LRU_C * r_t * jax.nn.softplus(-lru_lambda.astype(f32))
    a_t = jnp.exp(log_a)
    mult = jnp.sqrt(-jnp.expm1(2.0 * log_a))
    h = linear_scan(a_t, mult * (i_t * xb.astype(f32)))
    y_lru = h.astype(u.dtype) * jax.nn.gelu(lg)

    cu = ca * jax.nn.sigmoid(cb)
    cu = causal_dwconv(cu, cv_dw_w, cv_dw_b)
    y_cv = jax.nn.silu(layernorm(cu, cv_ln_g, cv_ln_b))

    merged = (jax.nn.sigmoid(g_a) * (y_hg @ w_branch[0])
              + jax.nn.sigmoid(g_b) * (y_lru @ w_branch[1])
              + jax.nn.sigmoid(g_c) * (y_cv @ w_branch[2]))
    return merged @ w_out

def first_inputs(seed: int = 0) -> dict:
    key = jax.random.key(seed)
    ks = jax.random.split(key, 24)
    L, D = DEPTH, D_MODEL

    def nrm(k, shape, fan_in):
        return jax.random.normal(k, shape, jnp.float32) * (fan_in ** -0.5)

    def gain(k, shape):
        return 1.0 + 0.01 * jax.random.normal(k, shape, jnp.float32)

    a_c = jax.random.uniform(ks[14], (L, LRU_WIDTH), jnp.float32, minval=0.9, maxval=0.999)
    sig = a_c ** (1.0 / LRU_C)
    lru_lambda = jnp.log(sig) - jnp.log1p(-sig)

    return {
        "x": jax.random.normal(ks[0], (BATCH, SEQ, D), jnp.float32),
        "norm_ffn1": gain(ks[1], (L, D)),
        "ffn1_w_in": nrm(ks[2], (L, D, 2 * D_FF), D),
        "ffn1_w_out": nrm(ks[3], (L, D_FF, D), D_FF),
        "norm_mix": gain(ks[4], (L, D)),
        "w_in_mix": nrm(ks[5], (L, D, MIX_COLS), D),
        "b_in_mix": 0.01 * jax.random.normal(ks[6], (L, MIX_COLS), jnp.float32),
        "hgrn_lb_logits": 0.5 * jax.random.normal(ks[7], (L, HG_WIDTH), jnp.float32),
        "hg_norm": gain(ks[8], (L, HG_HEAD_DIM)),
        "lru_conv_w": nrm(ks[9], (L, LRU_CONV, LRU_WIDTH), LRU_CONV),
        "lru_conv_b": 0.01 * jax.random.normal(ks[10], (L, LRU_WIDTH), jnp.float32),
        "lru_gate_w": nrm(ks[11], (L, 2, LRU_HEADS, LRU_HEAD_DIM, LRU_HEAD_DIM), LRU_HEAD_DIM),
        "lru_gate_b": 0.01 * jax.random.normal(ks[12], (L, 2, LRU_WIDTH), jnp.float32),
        "lru_lambda": lru_lambda,
        "cv_dw_w": nrm(ks[15], (L, CONV_KERNEL, CONV_WIDTH), CONV_KERNEL),
        "cv_dw_b": 0.01 * jax.random.normal(ks[16], (L, CONV_WIDTH), jnp.float32),
        "cv_ln_g": gain(ks[17], (L, CONV_WIDTH)),
        "cv_ln_b": 0.01 * jax.random.normal(ks[18], (L, CONV_WIDTH), jnp.float32),
        "w_branch": nrm(ks[19], (L, N_BRANCH, D, D), D),
        "w_out_mix": nrm(ks[20], (L, D, D), D),
        "norm_ffn2": gain(ks[21], (L, D)),
        "ffn2_w_in": nrm(ks[22], (L, D, 2 * D_FF), D),
        "ffn2_w_out": nrm(ks[23], (L, D_FF, D), D_FF),
        "norm_final": gain(ks[13], (D,)),
    }

def first_block(x, norm_ffn1, ffn1_w_in, ffn1_w_out, norm_mix, w_in_mix, b_in_mix, hgrn_lb_logits,
              hg_norm, lru_conv_w, lru_conv_b, lru_gate_w, lru_gate_b, lru_lambda, cv_dw_w, cv_dw_b,
              cv_ln_g, cv_ln_b, w_branch, w_out_mix, norm_ffn2, ffn2_w_in, ffn2_w_out, norm_final):
    lb_all = jax.nn.softmax(hgrn_lb_logits.astype(jnp.float32), axis=0)
    lb_all = jnp.cumsum(lb_all, axis=0) - lb_all[:1]
    for l in range(DEPTH):
        x = x + 0.5 * swiglu_ffn(rmsnorm(x, norm_ffn1[l]), ffn1_w_in[l], ffn1_w_out[l])
        x = x + hybrid_mixer(rmsnorm(x, norm_mix[l]), lb_all[l], w_in_mix[l], b_in_mix[l],
                             hg_norm[l], lru_conv_w[l], lru_conv_b[l], lru_gate_w[l], lru_gate_b[l],
                             lru_lambda[l], cv_dw_w[l], cv_dw_b[l], cv_ln_g[l], cv_ln_b[l],
                             w_branch[l], w_out_mix[l])
        x = x + 0.5 * swiglu_ffn(rmsnorm(x, norm_ffn2[l]), ffn2_w_in[l], ffn2_w_out[l])
    return rmsnorm(x, norm_final)


_first_inputs = first_inputs


def first_inputs(seed=0):
    import zlib

    import numpy as np

    out = dict(_first_inputs(seed))
    spreads = {}
    factors = {'norm_ffn1': 8.0,
     'norm_mix': 8.0,
     'b_in_mix': 3.467,
     'hg_norm': 8.0,
     'lru_conv_b': 4.072,
     'lru_gate_b': 8.0,
     'cv_dw_b': 8.0,
     'cv_ln_g': 8.0,
     'cv_ln_b': 8.0,
     'norm_ffn2': 8.0,
     'norm_final': 5.495}
    for name, (base, spread) in spreads.items():
        noise = np.random.default_rng([zlib.crc32(name.encode()), seed]).standard_normal(out[name].shape)
        drawn = base * np.exp(spread * noise) if base else spread * noise
        out[name] = __import__('jax').numpy.asarray(drawn.astype(out[name].dtype))
    for name, factor in factors.items():
        out[name] = (out[name] * factor).astype(out[name].dtype)
    return out


_narrow_inputs = first_inputs


def first_inputs(seed=0):

    out = dict(_narrow_inputs(seed))
    wider = {'norm_mix': 3.54,
     'b_in_mix': 4.27,
     'hg_norm': 8.07,
     'lru_conv_b': 4.54,
     'lru_gate_b': 9.31,
     'cv_dw_b': 12.0,
     'cv_ln_g': 12.0,
     'cv_ln_b': 12.0,
     'norm_ffn2': 9.62,
     'norm_final': 6.17}
    for name, times in wider.items():
        mean = out[name].mean()
        out[name] = (mean + times * (out[name] - mean)).astype(out[name].dtype)
    return out


GRID_W = 64
CTX_LEN = 256

A_HEADS = 8
A_HEAD_DIM = 64
D_A = A_HEADS * A_HEAD_DIM
LORA_W = 64
LORA_A = 64
LORA_G = 128

B_HEADS = 8
B_HEAD_DIM = 64
D_B = B_HEADS * B_HEAD_DIM
WIN_H = 8
WIN_W = 16

N_EXPERTS = 16
N_GROUPS = 4
EXPERTS_PER_GROUP = N_EXPERTS // N_GROUPS
TOP_K = 2
D_EXPERT = 512

RMS_EPS = 1e-6
GN_EPS = 64e-5

IN_SPLITS = (D_A, D_A, D_A, 2 * LORA_W, 2 * LORA_A, LORA_G, D_B, D_B, D_B, D_MODEL, D_MODEL)
IN_COLS = sum(IN_SPLITS)
IN_OFFSETS = tuple(int(o) for o in np.cumsum(IN_SPLITS)[:-1])


def rms_norm(x, g):
    xf = x.astype(jnp.float32)
    y = xf * lax.rsqrt(jnp.mean(xf * xf, axis=-1, keepdims=True) + RMS_EPS)
    return (y * g.astype(jnp.float32)).astype(x.dtype)

def modulate(h, shift, scale):
    return h * (1.0 + scale) + shift

def split_cols(z):
    return jnp.split(z, IN_OFFSETS, axis=-1)

def rwkv_prep(z, w0, w_lora_b, a0, a_lora_b, k_k, k_a):
    f = jnp.float32
    k, v, lw, la = z[1].astype(f), z[2].astype(f), z[3].astype(f), z[4].astype(f)
    bsz, t = k.shape[:2]
    heads = lambda u: u.reshape(bsz, t, A_HEADS, A_HEAD_DIM)
    lw = jnp.tanh(lw).reshape(bsz, t, 2, LORA_W)
    wl = w0.astype(f) + jnp.einsum('btzr,zrc->btzc', lw, w_lora_b.astype(f))
    decay = jnp.exp(-jnp.exp(-jax.nn.softplus(-wl) - 0.5))
    la = la.reshape(bsz, t, 2, LORA_A)
    a = jax.nn.sigmoid(a0.astype(f) + jnp.einsum('btzr,zrc->btzc', la, a_lora_b.astype(f)))
    kk = heads(k * k_k.astype(f))
    kk = kk * lax.rsqrt(jnp.maximum(jnp.sum(kk * kk, axis=-1, keepdims=True), 1e-12))
    k_dir = k[:, :, None, :] * (1.0 + (a - 1.0) * k_a.astype(f))
    per_dir = [(heads(decay[:, :, d]), heads(k_dir[:, :, d]), heads(a[:, :, d])) for d in range(2)]
    return heads(k), heads(v), kk, per_dir

def rwkv_scan(s0, r, decay, k, v, kk, a, reverse, emit):
    def step(s, inp):
        w_t, k_t, v_t, kk_t, a_t = inp[:5]
        s_kk = jnp.einsum('bhvk,bhk->bhv', s, kk_t)
        s = (s * w_t[:, :, None, :]
             - s_kk[..., None] * (kk_t * a_t)[:, :, None, :]
             + v_t[..., None] * k_t[:, :, None, :])
        y = jnp.einsum('bhvk,bhk->bhv', s, inp[5]) if emit else None
        return s, y
    seq = (decay, k, v, kk, a) + ((r,) if emit else ())
    xs = tuple(jnp.moveaxis(u, 1, 0) for u in seq)
    s_final, ys = lax.scan(step, s0, xs, reverse=reverse)
    return s_final, (jnp.moveaxis(ys, 0, 1) if emit else None)

def rwkv_out(y, r, k, v, lg, r_k, g_lora_b, ln_g, ln_b, out_dtype):
    f = jnp.float32
    bsz, t = y.shape[:2]
    mu = jnp.mean(y, axis=-1, keepdims=True)
    var = jnp.mean(jnp.square(y - mu), axis=-1, keepdims=True)
    yn = ((y - mu) * lax.rsqrt(var + GN_EPS)).reshape(bsz, t, D_A) * ln_g.astype(f) + ln_b.astype(f)
    bonus = (jnp.sum(r * k * r_k.astype(f), axis=-1, keepdims=True) * v).reshape(bsz, t, D_A)
    g = jax.nn.sigmoid(lg.astype(f)) @ g_lora_b.astype(f)
    return ((yn + bonus) * g).astype(out_dtype)

def rwkv_mixer(z_c, z_x, w0, w_lora_b, a0, a_lora_b, g_lora_b, k_k, k_a, r_k, ln_g, ln_b, emit_ctx):
    f = jnp.float32
    k_c, v_c, kk_c, dir_c = rwkv_prep(z_c, w0, w_lora_b, a0, a_lora_b, k_k, k_a)
    k_x, v_x, kk_x, dir_x = rwkv_prep(z_x, w0, w_lora_b, a0, a_lora_b, k_k, k_a)
    bsz, seq = z_x[0].shape[:2]
    r_x = z_x[0].astype(f).reshape(bsz, seq, A_HEADS, A_HEAD_DIM)
    r_c = z_c[0].astype(f).reshape(bsz, z_c[0].shape[1], A_HEADS, A_HEAD_DIM) if emit_ctx else None
    y_x, y_c = 0.0, 0.0
    for d in range(2):
        rev = d == 1
        s0 = jnp.zeros((bsz, A_HEADS, A_HEAD_DIM, A_HEAD_DIM), f)
        w_c, kd_c, a_c = dir_c[d]
        s_c, yc_d = rwkv_scan(s0, r_c, w_c, kd_c, v_c, kk_c, a_c, rev, emit_ctx)
        w_x, kd_x, a_x = dir_x[d]
        _, yx_d = rwkv_scan(s_c, r_x, w_x, kd_x, v_x, kk_x, a_x, rev, True)
        y_x = y_x + yx_d
        if emit_ctx:
            y_c = y_c + yc_d
    out_x = rwkv_out(y_x, r_x, k_x, v_x, z_x[5], r_k, g_lora_b, ln_g, ln_b, z_x[0].dtype)
    out_c = rwkv_out(y_c, r_c, k_c, v_c, z_c[5], r_k, g_lora_b, ln_g, ln_b, z_c[0].dtype) if emit_ctx else None
    return out_c, out_x

def na_mixer(z_c, z_x, q_g, k_g, rpb, need_ctx):
    f = jnp.float32
    scale = B_HEAD_DIM ** -0.5

    def heads(u):
        bsz, t = u.shape[:2]
        return u.reshape(bsz, t, B_HEADS, B_HEAD_DIM).transpose(0, 2, 1, 3)

    k_c, v_c = rms_norm(heads(z_c[7]), k_g), heads(z_c[8])
    q_x = rms_norm(heads(z_x[6]), q_g) * scale
    k_x, v_x = rms_norm(heads(z_x[7]), k_g), heads(z_x[8])
    bsz, _, seq, _ = q_x.shape
    rows = seq // GRID_W
    kh = min(WIN_H, rows)
    kw = WIN_W
    grid = lambda u: u.reshape(bsz, B_HEADS, rows, GRID_W, B_HEAD_DIM)
    q_grid, k_grid, v_grid = grid(q_x), grid(k_x), grid(v_x)

    i = jnp.arange(rows)
    key_rows = jnp.clip(i - kh // 2, 0, rows - kh)[:, None] + jnp.arange(kh)[None, :]
    k_blk = k_grid[:, :, key_rows]
    v_blk = v_grid[:, :, key_rows]
    s_lat = jnp.einsum('bhiqd,bhiakd->bhiqak', q_grid, k_blk).astype(f)

    j = jnp.arange(GRID_W)
    col_start = jnp.clip(j - kw // 2, 0, GRID_W - kw)
    in_win = (j[None, :] >= col_start[:, None]) & (j[None, :] < col_start[:, None] + kw)
    d_row = key_rows - i[:, None] + (WIN_H - 1)
    d_col = jnp.clip(j[None, :] - j[:, None], -(WIN_W - 1), WIN_W - 1) + (WIN_W - 1)
    bias = rpb[:, d_row[:, None, :, None], d_col[None, :, None, :]].astype(f)
    s_lat = jnp.where(in_win[:, None, :], s_lat + bias[None], -jnp.inf)

    s_ctx = jnp.einsum('bhiqd,bhcd->bhiqc', q_grid, k_c).astype(f)
    n_lat = kh * GRID_W
    logits = jnp.concatenate([s_lat.reshape(bsz, B_HEADS, rows, GRID_W, n_lat), s_ctx], axis=-1)
    p = jax.nn.softmax(logits, axis=-1).astype(v_x.dtype)
    p_lat = p[..., :n_lat].reshape(bsz, B_HEADS, rows, GRID_W, kh, GRID_W)
    o = (jnp.einsum('bhiqak,bhiakd->bhiqd', p_lat, v_blk)
         + jnp.einsum('bhiqc,bhcd->bhiqd', p[..., n_lat:], v_c))
    y_x = o.transpose(0, 2, 3, 1, 4).reshape(bsz, seq, D_B)

    y_c = None
    if need_ctx:
        q_c = rms_norm(heads(z_c[6]), q_g) * scale
        p_c = jax.nn.softmax(jnp.einsum('bhqd,bhkd->bhqk', q_c, k_c).astype(f), axis=-1).astype(v_c.dtype)
        y_c = jnp.einsum('bhqk,bhkd->bhqd', p_c, v_c).transpose(0, 2, 1, 3).reshape(bsz, -1, D_B)
    return y_c, y_x

def branch_merge(gate_a, gate_b, y_a, y_b, proj_a, proj_b, w_out):
    merged = jax.nn.sigmoid(gate_a) * (y_a @ proj_a) + jax.nn.sigmoid(gate_b) * (y_b @ proj_b)
    return merged @ w_out

def moe(h, router_w, router_bias, w1, w3, w2):
    f = jnp.float32
    shp = h.shape
    t = h.reshape(-1, shp[-1])
    n = t.shape[0]
    scores = jax.nn.sigmoid(t.astype(f) @ router_w.astype(f))
    sel = scores + router_bias.astype(f)
    grp_score = lax.top_k(sel.reshape(n, N_GROUPS, EXPERTS_PER_GROUP), TOP_K)[0].sum(-1)
    best = jnp.argmax(grp_score, axis=-1)
    in_group = (jnp.arange(N_EXPERTS) // EXPERTS_PER_GROUP)[None, :] == best[:, None]
    _, top_idx = lax.top_k(jnp.where(in_group, sel, -jnp.inf), TOP_K)
    top_s = jnp.take_along_axis(scores, top_idx, axis=-1)
    wts = top_s / jnp.sum(top_s, axis=-1, keepdims=True)
    gate = jnp.sum(jax.nn.one_hot(top_idx, N_EXPERTS, dtype=f) * wts[..., None], axis=1).astype(t.dtype)
    out = jnp.zeros_like(t)
    for e in range(N_EXPERTS):
        hid = jax.nn.silu(t @ w1[e]) * (t @ w3[e])
        out = out + gate[:, e:e + 1] * (hid @ w2[e])
    return out.reshape(shp)

def second_inputs(seed: int = 0) -> dict:
    key = jax.random.key(seed)
    ks = iter(jax.random.split(key, 40))
    D = D_MODEL

    def nrm(shape, s):
        return jax.random.normal(next(ks), shape, jnp.float32) * s

    inp = {}
    inp['x'] = nrm((BATCH, SEQ, D), 1.0)
    inp['c'] = nrm((BATCH, D), 1.0)
    inp['ctx'] = nrm((BATCH, CTX_LEN, D), 1.0)
    inp['c_ctx'] = nrm((D,), 1.0)
    inp['mod_w'] = nrm((DEPTH, D, 6 * D), 0.5 * D ** -0.5)
    inp['mod_b'] = nrm((DEPTH, 6 * D), 0.02)
    inp['norm1_g'] = 1.0 + nrm((DEPTH, D), 0.05)
    inp['norm2_g'] = 1.0 + nrm((DEPTH, D), 0.05)
    inp['w_in'] = nrm((DEPTH, D, IN_COLS), D ** -0.5)
    inp['rw_w0'] = jax.random.uniform(next(ks), (DEPTH, 2, D_A), jnp.float32, -6.0, 1.0)
    inp['rw_w_lora_b'] = nrm((DEPTH, 2, LORA_W, D_A), 0.5 * LORA_W ** -0.5)
    inp['rw_a0'] = nrm((DEPTH, 2, D_A), 0.5)
    inp['rw_a_lora_b'] = nrm((DEPTH, 2, LORA_A, D_A), 0.5 * LORA_A ** -0.5)
    inp['rw_g_lora_b'] = nrm((DEPTH, LORA_G, D_A), LORA_G ** -0.5)
    inp['rw_k_k'] = 0.85 + nrm((DEPTH, D_A), 0.05)
    inp['rw_k_a'] = 1.0 + nrm((DEPTH, D_A), 0.05)
    inp['rw_r_k'] = nrm((DEPTH, A_HEADS, A_HEAD_DIM), 0.1)
    inp['rw_ln_g'] = 1.0 + nrm((DEPTH, D_A), 0.05)
    inp['rw_ln_b'] = nrm((DEPTH, D_A), 0.02)
    inp['na_q_g'] = 1.0 + nrm((DEPTH, B_HEAD_DIM), 0.1)
    inp['na_k_g'] = 1.0 + nrm((DEPTH, B_HEAD_DIM), 0.1)
    inp['na_rpb'] = nrm((DEPTH, B_HEADS, 2 * WIN_H - 1, 2 * WIN_W - 1), 0.5)
    inp['proj_a'] = nrm((DEPTH, D_A, D), D_A ** -0.5)
    inp['proj_b'] = nrm((DEPTH, D_B, D), D_B ** -0.5)
    inp['w_out'] = nrm((DEPTH, D, D), D ** -0.5)
    inp['router_w'] = nrm((D, N_EXPERTS), D ** -0.5)
    inp['router_bias'] = nrm((N_EXPERTS,), 0.01)
    inp['moe_w1'] = nrm((DEPTH, N_EXPERTS, D, D_EXPERT), D ** -0.5)
    inp['moe_w3'] = nrm((DEPTH, N_EXPERTS, D, D_EXPERT), D ** -0.5)
    inp['moe_w2'] = nrm((DEPTH, N_EXPERTS, D_EXPERT, D), D_EXPERT ** -0.5)
    return inp

def second_block(x, c, ctx, c_ctx, mod_w, mod_b, norm1_g, norm2_g, w_in,
              rw_w0, rw_w_lora_b, rw_a0, rw_a_lora_b, rw_g_lora_b, rw_k_k, rw_k_a, rw_r_k,
              rw_ln_g, rw_ln_b, na_q_g, na_k_g, na_rpb, proj_a, proj_b, w_out,
              router_w, router_bias, moe_w1, moe_w3, moe_w2):
    for l in range(DEPTH):
        last = l == DEPTH - 1
        m_x = [m[:, None, :] for m in jnp.split(jax.nn.silu(c) @ mod_w[l] + mod_b[l], 6, axis=-1)]
        m_c = jnp.split(jax.nn.silu(c_ctx) @ mod_w[l] + mod_b[l], 6, axis=-1)

        h_x = modulate(rms_norm(x, norm1_g[l]), m_x[0], m_x[1])
        h_c = modulate(rms_norm(ctx, norm1_g[l]), m_c[0], m_c[1])
        z_x = split_cols(h_x @ w_in[l])
        z_c = split_cols(h_c @ w_in[l])
        ya_c, ya_x = rwkv_mixer(z_c, z_x, rw_w0[l], rw_w_lora_b[l], rw_a0[l], rw_a_lora_b[l],
                                rw_g_lora_b[l], rw_k_k[l], rw_k_a[l], rw_r_k[l], rw_ln_g[l], rw_ln_b[l],
                                emit_ctx=not last)
        yb_c, yb_x = na_mixer(z_c, z_x, na_q_g[l], na_k_g[l], na_rpb[l], need_ctx=not last)
        x = x + m_x[2] * branch_merge(z_x[9], z_x[10], ya_x, yb_x, proj_a[l], proj_b[l], w_out[l])

        h2_x = modulate(rms_norm(x, norm2_g[l]), m_x[3], m_x[4])
        x = x + m_x[5] * moe(h2_x, router_w, router_bias, moe_w1[l], moe_w3[l], moe_w2[l])

        if not last:
            ctx = ctx + m_c[2] * branch_merge(z_c[9], z_c[10], ya_c, yb_c, proj_a[l], proj_b[l], w_out[l])
            h2_c = modulate(rms_norm(ctx, norm2_g[l]), m_c[3], m_c[4])
            ctx = ctx + m_c[5] * moe(h2_c, router_w, router_bias, moe_w1[l], moe_w3[l], moe_w2[l])
    return x


def setup_inputs(seed=0):
    out = dict(first_inputs(seed))
    for name, value in second_inputs(seed + 1).items():
        if name != "x":
            out[name + "_2"] = value
    return out


def reference(
    x, norm_ffn1, ffn1_w_in, ffn1_w_out, norm_mix, w_in_mix, b_in_mix, hgrn_lb_logits, hg_norm,
    lru_conv_w, lru_conv_b, lru_gate_w, lru_gate_b, lru_lambda, cv_dw_w, cv_dw_b, cv_ln_g,
    cv_ln_b, w_branch, w_out_mix, norm_ffn2, ffn2_w_in, ffn2_w_out, norm_final, c_2, ctx_2,
    c_ctx_2, mod_w_2, mod_b_2, norm1_g_2, norm2_g_2, w_in_2, rw_w0_2, rw_w_lora_b_2, rw_a0_2,
    rw_a_lora_b_2, rw_g_lora_b_2, rw_k_k_2, rw_k_a_2, rw_r_k_2, rw_ln_g_2, rw_ln_b_2, na_q_g_2,
    na_k_g_2, na_rpb_2, proj_a_2, proj_b_2, w_out_2, router_w_2, router_bias_2, moe_w1_2,
    moe_w3_2, moe_w2_2,
):
    x = first_block(
        x, norm_ffn1, ffn1_w_in, ffn1_w_out, norm_mix, w_in_mix, b_in_mix, hgrn_lb_logits,
        hg_norm, lru_conv_w, lru_conv_b, lru_gate_w, lru_gate_b, lru_lambda, cv_dw_w, cv_dw_b,
        cv_ln_g, cv_ln_b, w_branch, w_out_mix, norm_ffn2, ffn2_w_in, ffn2_w_out, norm_final,
    )
    return second_block(
        x, c_2, ctx_2, c_ctx_2, mod_w_2, mod_b_2, norm1_g_2, norm2_g_2, w_in_2, rw_w0_2,
        rw_w_lora_b_2, rw_a0_2, rw_a_lora_b_2, rw_g_lora_b_2, rw_k_k_2, rw_k_a_2, rw_r_k_2,
        rw_ln_g_2, rw_ln_b_2, na_q_g_2, na_k_g_2, na_rpb_2, proj_a_2, proj_b_2, w_out_2,
        router_w_2, router_bias_2, moe_w1_2, moe_w3_2, moe_w2_2,
    )


_drawn_inputs = setup_inputs


def setup_inputs(seed=0):
    import zlib

    import numpy as np

    out = dict(_drawn_inputs(seed))
    spreads = {}
    factors = {'cv_dw_b': 3.132,
     'cv_ln_g': 4.837,
     'cv_ln_b': 4.827,
     'ctx_2': 8.0,
     'c_ctx_2': 8.0,
     'mod_b_2': 8.0,
     'norm1_g_2': 8.0,
     'norm2_g_2': 37.686,
     'rw_w0_2': 43.512,
     'rw_w_lora_b_2': 64.0,
     'rw_a0_2': 64.0,
     'rw_a_lora_b_2': 64.0,
     'rw_k_k_2': 64.0,
     'rw_k_a_2': 64.0,
     'rw_r_k_2': 3.138,
     'rw_ln_g_2': 64.0,
     'rw_ln_b_2': 64.0,
     'na_q_g_2': 8.0,
     'na_k_g_2': 8.0,
     'na_rpb_2': 8.0,
     'proj_b_2': 7.306,
     'router_bias_2': 8.0}
    for name, (base, spread) in spreads.items():
        noise = np.random.default_rng([zlib.crc32(name.encode()), seed]).standard_normal(out[name].shape)
        drawn = base * np.exp(spread * noise) if base else spread * noise
        out[name] = jnp.asarray(drawn.astype(out[name].dtype))
    for name, factor in factors.items():
        out[name] = (out[name] * factor).astype(out[name].dtype)
    return out
```

```python
from contextlib import ExitStack

import numpy as np

import concourse.bass as bass
from concourse import mybir

ALU = mybir.AluOpType
ACT = mybir.ActivationFunctionType
AX = mybir.AxisListType
F32 = mybir.dt.float32
U32 = mybir.dt.uint32
F32R = mybir.dt.float32r

P = 128
T = 512
TC = 256
TA = T + TC
D = 1024
DT = D // P
FF = 2816
FT = FF // P
HEADS = 8
SLAB = 8
RING = 4
E = 16
DE = 512
LEVELS = (64, 32, 16, 8, 4, 2, 1)
CONV = 31

PAR = [
    ("norm_ffn1", DT), ("norm_mix", DT), ("norm_ffn2", DT), ("norm_final", DT), ("norm1", DT), ("norm2", DT),
    ("b_mix", 88), ("lb_logits", DT), ("hg_norm", 1), ("lru_conv_w", 4 * DT), ("lru_conv_b", DT),
    ("gate_b", 2 * DT), ("lambda", DT), ("cv_w", CONV * DT), ("cv_b", DT), ("cv_ln_g", DT), ("cv_ln_b", DT),
    ("mod_b", 48), ("w0", 8), ("a0", 8), ("k_k", 4), ("k_a", 4), ("r_k", 4), ("ln_g", 4), ("ln_b", 4),
    ("q_g", 1), ("k_g", 1), ("c", 2 * DT),
]
PAR_AT = {}
_at = 0
for _n, _c in PAR:
    PAR_AT[_n] = _at
    _at += _c
NPAR = _at

PARTS = [("ffn1_in", 2 * FT), ("ffn1_out", FT), ("hgrn", 4 * HEADS), ("lru", 4 * DT), ("merge", 6 * DT),
         ("mix_out", DT), ("ffn2_in", 2 * FT), ("ffn2_out", FT), ("mod", 48), ("in2", 23), ("v2", 4),
         ("merge2", 3 * DT), ("out2", DT), ("moe", 12 * E)]
SLAB_AT = {}
_at = 0
for _n, _c in PARTS:
    SLAB_AT[_n] = _at
    _at += _c
N_SLABS = _at

SPLIT_AT = {"ffn1_in": 0, "ffn1_out": 2 * FT, "ffn2_in": 3 * FT, "ffn2_out": 5 * FT, "moe": 6 * FT}


class Steps:

    def __init__(self, sem, names, base=0):
        self.sem, self.names, self.base = sem, names.split(), base
        assert len(set(self.names)) == len(self.names)

    def at(self, unit, name):
        return unit * len(self.names) + (self.base + self.names.index(name) + 1)

    def end(self, units):
        return self.base + units * len(self.names)


def hybrid_block_kernel(nc, stream, par, x_t, vbias, gate_w, masks, ctx_t, rpb, router_w, lora, spill, gates_dram, out):
    ctx = ExitStack()
    with ctx:
        def sb(name, shape, dt=F32):
            return ctx.enter_context(nc.sbuf_tensor(name, shape, dt))

        def sem(name):
            return ctx.enter_context(nc.semaphore(name))

        def both_types(name, shape):
            at = (nc.sbuf_base + 31) // 32 * 32
            plain = sb(name, shape)
            return plain, nc.alloc_sbuf_tensor_at(name + "_r", shape, F32R, offset=at)

        ring, ring_r = both_types("ring", [P, RING, SLAB, P])
        resid = sb("resid", [P, DT, T])
        xn, xn_r = both_types("xn", [P, DT, T])
        pv = sb("pv", [P, NPAR])
        negpv = sb("negpv", [P, 1])
        ones = sb("ones", [P, P])
        ident = sb("ident", [P, P])
        shared = sb("shared", [P, 2432])
        same_block = shared[:, 0:7 * P].rearrange("p (l t) -> p l t", l=7)
        chunk_start = shared[:, 7 * P:11 * P]
        eps = sb("eps", [P, 6])
        lb = sb("lb", [P, 2, DT])
        lru_c = sb("lru_c", [P, DT])
        std = sb("std", [P, T])
        scr = sb("scr", [P, 32])
        mem_at = (nc.sbuf_base + 31) // 32 * 32
        mem = sb("mem", [P, 69 * T])

        def part_of_mem(name, first, shape, dt=F32R):
            return nc.alloc_sbuf_tensor_at(name, [P] + shape, dt, offset=mem_at + 4 * first)

        big = mem[:, 0:32 * T].rearrange("p (b a t) -> p b a t", b=4, a=DT)
        work = mem[:, 32 * T:69 * T]
        hid_hi = part_of_mem("hid_hi", 0, [FT, T])
        hid_lo = part_of_mem("hid_lo", FT * T, [FT, T])
        ffn_xh = part_of_mem("ffn_xh", 2 * FT * T, [DT, T])
        whi = part_of_mem("whi", 61 * T, [RING, SLAB, P])
        y_hg, y_lru, y_cv, merged = (big[:, i, :, :] for i in range(4))
        gu = part_of_mem("gu", 52 * T, [2, T], F32)

        psum = ctx.enter_context(nc.psum_tensor("psum", [P, 8, T], F32))

        def col(name, i=0, n=1):
            a = PAR_AT[name]
            return pv[:, a + i:a + i + n] if isinstance(i, int) else pv[:, bass.ds(i + a, n)]

        slab_in = [sem(f"slab_in{r}") for r in range(RING)]
        slab_used = sem("slab_used")
        x_in = sem("x_in")
        par_in = sem("par_in")
        const_ready = sem("const_ready")
        setup = Steps(sem("setup_act"), "e lnu el")
        setup_v = Steps(sem("setup_dve"), "m t0 smx s1 lb omlb al u c sp0 sp1 sp2 sp3 sp4")
        sq_ready = sem("sq_ready")
        sum_ready = sem("sum_ready")
        std_ready = sem("std_ready")
        rstd_ready = sem("rstd_ready")
        xn_ready = sem("xn_ready")
        resid_ready = sem("resid_ready")
        w_hi = sem("w_hi")
        w_lo = sem("w_lo")
        x_hi = sem("x_hi")
        x_lo = sem("x_lo")
        hraw_ready = sem("hraw_ready")
        hhi_ready = sem("hhi_ready")
        sig_ready = sem("sig_ready")
        sg_ready = sem("sg_ready")
        hid_ready = sem("hid_ready")
        ffo_ready = sem("ffo_ready")

        def slab(part, j, i=0, per=0):
            g = SLAB_AT[part] + j
            assert per % RING == 0
            return g % RING, (g // RING + 1 + i * (per // RING)) * 16

        def use_slab(pe, part, j, i=0, per=0):
            s, v = slab(part, j, i, per)
            pe.wait_ge(slab_in[s], v)
            return ring[:, s, :, :]

        def f(ap):
            return ap.bitcast(F32)

        def split_hi(act, part, j, i=0, per=0):
            w = use_slab(act, part, j, i, per)
            act.activation(whi[:, (SLAB_AT[part] + j) % RING, :, :], w, ACT.Copy).then_inc(w_hi, 1)

        def split_lo(pool, part, j, i=0, per=0):
            s = (SLAB_AT[part] + j) % RING
            pool.wait_ge(w_hi, i * per + (SPLIT_AT[part] + j + 1))
            pool.tensor_tensor(ring_r[:, s, :, :], ring[:, s, :, :], f(whi[:, s, :, :]), ALU.subtract).then_inc(w_lo, 1)

        def use_split(pe, part, j, i=0, per=0):
            s = (SLAB_AT[part] + j) % RING
            pe.wait_ge(w_lo, i * per + (SPLIT_AT[part] + j + 1))
            return whi[:, s, :, :], ring_r[:, s, :, :]

        def product(pe, bank, w, b, x_hi_, x_lo_, start, stop):
            hi, lo = w
            pe.matmul(bank, lo[:, b, :], x_hi_, start=start, stop=False, skip_group_check=True)
            pe.matmul(bank, hi[:, b, :], x_hi_, start=False, stop=False, skip_group_check=True)
            return pe.matmul(bank, hi[:, b, :], x_lo_, start=False, stop=stop, skip_group_check=True)

        def x_hi_act(act, n, norms, xh):
            for j in range(DT):
                act.wait_ge(xn_ready, DT * norms + j + 1)
                act.activation(xh[:, j, :], xn[:, j, :], ACT.Copy).then_inc(x_hi, 1)

        def x_lo_dve(dve, n, xh):
            for j in range(DT):
                dve.wait_ge(x_hi, DT * n + j + 1)
                dve.tensor_tensor(xn_r[:, j, :], xn[:, j, :], f(xh[:, j, :]), ALU.subtract).then_inc(x_lo, 1)


        def start_pool(pool):
            pool.memset(ones[:, :], 1.0).then_inc(const_ready, 1)
            pool.memset(ident[:, :], 0.0).then_inc(const_ready, 1)
            pool.memset(same_block[:, :, :], 0.0).then_inc(const_ready, 1)
            pool.memset(chunk_start, 1.0).then_inc(const_ready, 1)
            pool.memset(eps[:, 0:1], 1e-6).then_inc(const_ready, 1)
            pool.memset(eps[:, 1:2], 1e-5).then_inc(const_ready, 1)
            pool.memset(eps[:, 2:3], 0.0).then_inc(const_ready, 1)
            pool.memset(eps[:, 3:4], 64e-6).then_inc(const_ready, 1)
            pool.memset(eps[:, 4:5], 64e-5).then_inc(const_ready, 1)
            pool.memset(eps[:, 5:6], 1e-12).then_inc(const_ready, 1)
            pool.wait_ge(const_ready, 10)
            n = 10
            pool.memset(chunk_start.rearrange("p (c t) -> p c t", t=P)[:, :, 0:1], 0.0).then_inc(const_ready, 1)
            pool.affine_select(out=ident[:, :], in_=ident[:, :], compare_op=ALU.not_equal, fill=1.0, base=0,
                               pattern=[[-1, P]], channel_multiplier=1).then_inc(const_ready, 1)
            n += 2
            for li, L in enumerate(LEVELS):
                right = same_block[:, li, :].rearrange("p (b h c) -> p b h c", h=2, c=L)[:, :, 1, :]
                pool.memset(right, 1.0).then_inc(const_ready, 1)
                pool.wait_ge(const_ready, n + 1)
                pool.affine_select(out=right, in_=right, compare_op=ALU.is_ge, fill=0.0, base=0,
                                   pattern=[[-2 * L, P // (2 * L)], [0, L]], channel_multiplier=1).then_inc(const_ready, 1)
                pool.wait_ge(const_ready, n + 2)
                pool.affine_select(out=right, in_=right, compare_op=ALU.is_ge, fill=0.0, base=L - 1,
                                   pattern=[[2 * L, P // (2 * L)], [0, L]], channel_multiplier=-1).then_inc(const_ready, 1)
                n += 3
            assert n == N_CONST, n

        N_CONST = 12 + 3 * len(LEVELS)

        def start_sync(sp):
            sp.dma_start(pv[:, :], par).then_inc(par_in, 16)
            sp.dma_start(resid[:, :, :], x_t).then_inc(x_in, 16)

        def stream_sync(sp):
            for r in range(RING):
                sp.dma_start(ring[:, r, :, :], stream[r]).then_inc(slab_in[r], 16)
            last = N_SLABS // RING * RING
            with sp.Fori(1, last // RING) as i:
                for r in range(RING):
                    sp.wait_ge(slab_used, i * RING + (r + 1 - RING))
                    sp.dma_start(ring[:, r, :, :], stream[i * RING + r]).then_inc(slab_in[r], 16)
            for g in range(last, N_SLABS):
                sp.wait_ge(slab_used, g + 1 - RING)
                sp.dma_start(ring[:, g % RING, :, :], stream[g]).then_inc(slab_in[g % RING], 16)

        def start_act(act):
            a, v = setup, setup_v
            act.wait_ge(v.sem, v.at(0, "t0"))
            act.activation(lb[:, 0, :], lb[:, 0, :], ACT.Exp).then_inc(a.sem, 1)
            act.wait_ge(v.sem, v.at(0, "al"))
            act.activation(lru_c[:, :], lru_c[:, :], ACT.Exp, scale=-1.0).then_inc(a.sem, 1)
            act.wait_ge(v.sem, v.at(0, "u"))
            act.activation(scr[:, 8:16], scr[:, 0:8], ACT.Ln).then_inc(a.sem, 1)

        def start_dve(dve):
            a, v = setup, setup_v
            dve.wait_ge(par_in, 16)
            lg = col("lb_logits", 0, DT)

            def step(ins, name):
                dve.wait_ge(v.sem, v.at(0, name))

            step(dve.tensor_copy(lb[:, 1, :], lg).then_inc(v.sem, 1), "m")
            dve.tensor_tensor(lb[:, 0, :], lg, lb[:, 1, :], ALU.subtract).then_inc(v.sem, 1)
            dve.wait_ge(a.sem, a.at(0, "e"))
            step(dve.reciprocal(lb[:, 1, :], lb[:, 0, :]).then_inc(v.sem, 1), "smx")
            step(dve.tensor_tensor(lb[:, 1, :], lb[:, 0, :], lb[:, 1, :], ALU.mult).then_inc(v.sem, 1), "s1")
            step(dve.tensor_tensor(lb[:, 0, :], lb[:, 1, :], lb[:, 1, :], ALU.subtract).then_inc(v.sem, 1), "lb")
            dve.tensor_scalar(lb[:, 1, :], lb[:, 0, :], -1.0, 1.0, ALU.mult, ALU.add).then_inc(v.sem, 1)
            lam = col("lambda", 0, DT)
            dve.scalar_tensor_tensor(lru_c[:, :], lam, -1.0, lam, ALU.mult, ALU.max).then_inc(v.sem, 1)
            dve.wait_ge(a.sem, a.at(0, "lnu"))
            step(dve.tensor_scalar(scr[:, 0:8], lru_c[:, :], 1.0, None, ALU.add).then_inc(v.sem, 1), "u")
            step(dve.scalar_tensor_tensor(scr[:, 16:24], scr[:, 0:8], -1.0, lru_c[:, :], ALU.add, ALU.subtract)
                 .then_inc(v.sem, 1), "c")
            step(dve.reciprocal(scr[:, 24:32], scr[:, 0:8]).then_inc(v.sem, 1), "sp0")
            step(dve.tensor_tensor(scr[:, 16:24], scr[:, 16:24], scr[:, 24:32], ALU.mult).then_inc(v.sem, 1), "sp1")
            dve.wait_ge(a.sem, a.at(0, "el"))
            step(dve.tensor_tensor(scr[:, 16:24], scr[:, 8:16], scr[:, 16:24], ALU.subtract).then_inc(v.sem, 1), "sp2")
            step(dve.scalar_tensor_tensor(scr[:, 16:24], lam, 0.0, scr[:, 16:24], ALU.min, ALU.subtract)
                 .then_inc(v.sem, 1), "sp3")
            dve.tensor_scalar(lru_c[:, :], scr[:, 16:24], 8.0, None, ALU.mult).then_inc(v.sem, 1)

        def norm_act(act, n, updates, ready=None):
            if updates:
                act.wait_ge(ready or resid_ready, updates)
            else:
                act.wait_ge(x_in, 16)
                act.wait_ge(const_ready, N_CONST)
            for j in range(DT):
                act.activation(xn[:, j, :], resid[:, j, :], ACT.Square).then_inc(sq_ready, 1)
            act.wait_ge(sum_ready, n + 1)
            act.activation(std[:, :], psum[:, 7, :], ACT.Sqrt, bias=eps[:, 0:1], scale=1.0 / D).then_inc(std_ready, 1)

        def norm_pe(pe, n):
            if n == 0:
                pe.wait_ge(const_ready, N_CONST)
            for j in range(DT):
                pe.wait_ge(sq_ready, DT * n + j + 1)
                ins = pe.matmul(psum[:, 7, :], ones[:, :], xn[:, j, :], start=j == 0, stop=j == DT - 1)
            ins.then_inc(sum_ready, 1)

        def norm_dve(dve, n, gain, target):
            dve.wait_ge(std_ready, n + 1)
            dve.reciprocal(std[:, :], std[:, :]).then_inc(rstd_ready, 1)
            dve.wait_ge(rstd_ready, n + 1)
            for j in range(DT):
                dve.scalar_tensor_tensor(target[:, j, :], resid[:, j, :], col(gain, j), std[:, :],
                                         ALU.mult, ALU.mult).then_inc(xn_ready, 1)

        def ffn_pe(pe, n):
            part = f"ffn{n + 1}_in"
            base = n * FT
            with pe.Fori(0, FT // 2) as i:
                for half in range(2):
                    pe.wait_ge(hid_ready, 2 * i + (base + half + 1))
                    for b in range(2):
                        w = use_split(pe, part, 2 * half + b, i, 4)
                        for k in range(DT):
                            if half == 0 and b == 0:
                                pe.wait_ge(x_lo, DT * n + k + 1)
                            ins = product(pe, psum[:, 2 * half + b, :], w, k, ffn_xh[:, k, :], xn_r[:, k, :],
                                          k == 0, k == DT - 1)
                        ins.then_inc(slab_used, 1)
            part = f"ffn{n + 1}_out"

            def out_slab(k, j, i, per, start, stop):
                w = use_split(pe, part, j, i, per)
                for m in range(DT):
                    ins = product(pe, psum[:, m, :], w, m, hid_hi[:, k, :], hid_lo[:, k, :], start, stop)
                ins.then_inc(slab_used, 1)

            pe.wait_ge(hid_ready, 2 + base + FT)
            out_slab(0, 0, 0, 0, True, False)
            out_slab(1, 1, 0, 0, False, False)
            with pe.Fori(0, 4) as i:
                for j in range(4):
                    out_slab(i * 4 + (2 + j), 2 + j, i, 4, False, False)
            for k in range(18, FT):
                out_slab(k, k, 0, 0, False, k == FT - 1)

        def ffn_act(act, n):
            base = n * FT
            part = f"ffn{n + 1}_in"
            split_hi(act, part, 0)
            split_hi(act, part, 1)
            x_hi_act(act, n, 2 * n, ffn_xh)
            with act.Fori(0, FT // 2) as i:
                for half in range(2):
                    split_hi(act, part, 2 * half + 2, i, 4)
                    split_hi(act, part, 2 * half + 3, i, 4)
                    act.wait_ge(slab_used, i * 4 + (SLAB_AT[part] + 2 * half + 2))
                    act.wait_ge(hid_ready, 2 * i + (base + half + 1))
                    act.activation(gu[:, half, :], psum[:, 2 * half, :], ACT.Sigmoid).then_inc(sig_ready, 1)
                    act.wait_ge(hraw_ready, 2 * i + (base + half + 1))
                    act.activation(hid_hi[:, 2 * i + half, :], gu[:, half, :], ACT.Copy).then_inc(hhi_ready, 1)
            with act.Fori(0, 5) as i:
                for j in range(4):
                    split_hi(act, f"ffn{n + 1}_out", 2 + j, i, 4)

        def ffn_pool(pool, n):
            part = f"ffn{n + 1}_in"
            with pool.Fori(0, 3 * FT // 4) as i:
                for j in range(4):
                    split_lo(pool, part, j, i, 4)
            for j in range(3 * FT // 4 * 4, 3 * FT):
                split_lo(pool, part, j)

        def ffn_dve(dve, n):
            base = n * FT
            x_lo_dve(dve, n, ffn_xh)
            with dve.Fori(0, FT // 2) as i:
                for half in range(2):
                    dve.wait_ge(sig_ready, 2 * i + (base + half + 1))
                    dve.tensor_tensor(gu[:, half, :], gu[:, half, :], psum[:, 2 * half, :], ALU.mult).then_inc(sg_ready, 1)
                    dve.wait_ge(sg_ready, 2 * i + (base + half + 1))
                    dve.tensor_tensor(gu[:, half, :], gu[:, half, :], psum[:, 2 * half + 1, :], ALU.mult).then_inc(hraw_ready, 1)
                    dve.wait_ge(hhi_ready, 2 * i + (base + half + 1))
                    dve.tensor_tensor(hid_lo[:, 2 * i + half, :], gu[:, half, :], f(hid_hi[:, 2 * i + half, :]),
                                      ALU.subtract).then_inc(hid_ready, 1)
            dve.wait_ge(slab_used, SLAB_AT[f"ffn{n + 1}_out"] + FT)
            for m in range(DT):
                dve.scalar_tensor_tensor(resid[:, m, :], psum[:, m, :], 0.5, resid[:, m, :],
                                         ALU.mult, ALU.add).then_inc(resid_ready, 1)

        WU = lambda u, n=1: work[:, u * T:(u + n) * T]
        ql = WU(0, 7).rearrange("p (l t) -> p l t", l=7)
        kl = WU(7, 7).rearrange("p (l t) -> p l t", l=7)
        dl = WU(14, 7).rearrange("p (l t) -> p l t", l=7)
        hq, hgl, hz, hlf, hk, hB, hqd, hkd, hv_tok, hkdT, hsc, hst, ho, hl1, he1, hEB = (WU(21 + n) for n in range(16))
        hst3 = hst[:, 0:3 * P].rearrange("p (c v) -> p c v", v=P)
        hi = Steps(sem("hgrn_pe"), "kdt s0 s1 kv s2 s3 s4 s5 s6 s7 o ss", 12)
        ha = Steps(sem("hgrn_act"), "sgq sgg az e l1 sn e1 l2 EB Ekd E0 E1 kdT osq lnss rstd", 16)
        hv = Steps(sem("hgrn_dve"), "qh gh z V lf t1 zc lf2 kh B dk " + " ".join(f"dr{i} dl{i}" for i in range(7))
                   + " qd kd " + " ".join(f"qm{i} km{i}" for i in range(7))
                   + " c0 c1 S1 S2 S3 c2 c3 c4 c5 c6 c7 y1 y2")
        hv.base = len(hv.names)
        hz_ready = sem("hgrn_zeros")
        vb_in = sem("vb_in")
        vb = shared[0:1, 11 * P:11 * P + D]
        tick = sb("tick", [P, 1])

        def halves(t, L):
            v = t.rearrange("p (b h c) -> p b h c", h=2, c=L)
            return v[:, :, 0, :], v[:, :, 1, :]

        def hgrn_pool(pool):
            pool.dma_start(vb, vbias).then_inc(vb_in, 16)
            pool.wait_ge(resid_ready, DT)
            pool.memset(ql, 0.0).then_inc(hz_ready, 1)
            pool.memset(kl, 0.0).then_inc(hz_ready, 1)

        def hgrn_proj(pe, h, static):
            j0, i = static
            for n, (bank, name, freed) in enumerate(((0, "q", "qh"), (1, "g", "gh"), (2, "f", "z"))):
                pe.wait_ge(hv.sem, hv.at(h - 1, freed))
                w = use_slab(pe, "hgrn", j0 + n, i, 4)
                for k in range(DT):
                    ins = pe.matmul(psum[:, bank, :], w[:, k, :], xn[:, k, :], start=k == 0, stop=k == DT - 1)
                    if k == 0:
                        first = ins
                ins.then_inc(slab_used, 1)
            pe.wait_ge(hv.sem, hv.at(h - 1, "V"))
            w = use_slab(pe, "hgrn", j0 + 3, i, 4)
            for c in range(4):
                pe.matmul(psum[:, 3, c * P:(c + 1) * P], ones[0:1, :], vb[:, bass.ds(h * P, P)], start=True, stop=False)
                for k in range(DT):
                    ins = pe.matmul(psum[:, 3, c * P:(c + 1) * P], xn[:, k, c * P:(c + 1) * P], w[:, k, :],
                                    start=False, stop=k == DT - 1)
            ins.then_inc(slab_used, 1)

        def proj_done(eng, h, n):
            eng.wait_ge(slab_used, h * 4 + (SLAB_AT["hgrn"] + n))

        def hgrn_scores(pe, h, li):
            bank = 5 + li % 2
            if li < 2:
                pe.wait_ge(hv.sem, hv.at(h - 1, f"c{6 + li}"))
                pe.wait_ge(ha.sem, ha.at(h - 1, "lnss"))
            else:
                pe.wait_ge(hv.sem, hv.at(h, f"c{li - 2}"))
            if li < 7:
                pe.wait_ge(hv.sem, hv.at(h, f"km{li}"))
                a, b = kl[:, li, :], ql[:, li, :]
            else:
                a, b = hk, hq
            for c in range(4):
                s = slice(c * P, (c + 1) * P)
                ins = pe.matmul(psum[:, bank, s], a[:, s], b[:, s], start=True, stop=True)
            ins.then_inc(hi.sem, 1)

        def hgrn_intra(pe, h):
            pe.wait_ge(hv.sem, hv.at(h, "kd"))
            pe.wait_ge(hv.sem, hv.at(h - 1, "y1"))
            for c in range(4):
                s = slice(c * P, (c + 1) * P)
                ins = pe.transpose(psum[:, 4, s], hkd[:, s], ident[:, :])
            ins.then_inc(hi.sem, 1)
            hgrn_scores(pe, h, 0)
            hgrn_scores(pe, h, 1)
            pe.wait_ge(ha.sem, ha.at(h, "kdT"))
            pe.wait_ge(hv.sem, hv.at(h - 1, "S3"))
            for c in range(3):
                s = slice(c * P, (c + 1) * P)
                ins = pe.matmul(psum[:, 7, s], hkdT[:, s], hv_tok[:, s], start=True, stop=True)
            ins.then_inc(hi.sem, 1)
            for li in range(2, 8):
                hgrn_scores(pe, h, li)
            pe.wait_ge(hv.sem, hv.at(h, "c7"))
            for c in range(4):
                s = slice(c * P, (c + 1) * P)
                ins = pe.matmul(psum[:, 4, s], hv_tok[:, s], hsc[:, s], start=True, stop=c == 0)
                if c:
                    ins = pe.matmul(psum[:, 4, s], hst3[:, c - 1, :], hqd[:, s], start=False, stop=True)
            ins.then_inc(hi.sem, 1)
            pe.wait_ge(ha.sem, ha.at(h, "osq"))
            pe.matmul(psum[:, 5, :], ones[:, :], ho, start=True, stop=True).then_inc(hi.sem, 1)

        def hgrn_pe(pe):
            pe.sem_inc(hi.sem, hi.base)
            pe.wait_ge(xn_ready, 2 * DT)
            pe.wait_ge(vb_in, 16)
            hgrn_proj(pe, 0, (0, 0))
            with pe.Fori(0, HEADS - 1) as h:
                hgrn_proj(pe, h + 1, (4, h))
                hgrn_intra(pe, h)
            hgrn_intra(pe, HEADS - 1)

        def hgrn_act(act):
            act.sem_inc(ha.sem, ha.base)
            with act.Fori(0, HEADS) as h:
                s, b = ha.sem, lambda n: pv[:, bass.ds(h + (PAR_AT["b_mix"] + n * DT), 1)]
                proj_done(act, h, 1)
                act.wait_ge(hi.sem, hi.at(h - 1, "s7"))
                act.activation(hq, psum[:, 0, :], ACT.Sigmoid, bias=b(0)).then_inc(s, 1)
                proj_done(act, h, 2)
                act.wait_ge(hv.sem, hv.at(h - 1, "y2"))
                act.activation(hgl, psum[:, 1, :], ACT.Sigmoid, bias=b(3)).then_inc(s, 1)
                act.wait_ge(hv.sem, hv.at(h, "z"))
                act.activation(he1, hz, ACT.Abs).then_inc(s, 1)
                act.wait_ge(s, ha.at(h, "az"))
                act.activation(he1, he1, ACT.Exp, scale=-1.0).then_inc(s, 1)
                act.wait_ge(s, ha.at(h, "e"))
                act.activation(hl1, he1, ACT.Ln, bias=ones[:, 0:1]).then_inc(s, 1)
                act.wait_ge(hv.sem, hv.at(h, "t1"))
                act.activation(hk, hl1, ACT.Exp, scale=-1.0).then_inc(s, 1)
                act.wait_ge(hv.sem, hv.at(h, "zc"))
                act.activation(he1, hz, ACT.Exp, scale=-1.0).then_inc(s, 1)
                act.wait_ge(s, ha.at(h, "e1"))
                act.activation(he1, he1, ACT.Ln, bias=ones[:, 0:1], scale=lb[:, 0, bass.ds(h, 1)]).then_inc(s, 1)
                act.wait_ge(hv.sem, hv.at(h, "B"))
                act.activation(hEB, hB, ACT.Exp).then_inc(s, 1)
                act.wait_ge(hv.sem, hv.at(h, "dk"))
                act.activation(hkd, hkd, ACT.Exp).then_inc(s, 1)
                act.wait_ge(hv.sem, hv.at(h, "dl3"))
                act.activation(dl[:, 0:4, :], dl[:, 0:4, :], ACT.Exp).then_inc(s, 1)
                act.wait_ge(hv.sem, hv.at(h, "dl6"))
                act.activation(dl[:, 4:7, :], dl[:, 4:7, :], ACT.Exp).then_inc(s, 1)
                act.wait_ge(hi.sem, hi.at(h, "kdt"))
                act.activation(hkdT, psum[:, 4, :], ACT.Copy).then_inc(s, 1)
                act.wait_ge(hi.sem, hi.at(h, "o"))
                act.activation(ho, psum[:, 4, :], ACT.Square).then_inc(s, 1)
                act.wait_ge(hi.sem, hi.at(h, "ss"))
                act.activation(hl1, psum[:, 5, :], ACT.Ln, bias=eps[:, 0:1], scale=1.0 / P).then_inc(s, 1)
                act.wait_ge(s, ha.at(h, "lnss"))
                act.activation(hl1, hl1, ACT.Exp, scale=-0.5).then_inc(s, 1)

        def hgrn_dve(dve):
            s = hv.sem
            dve.sem_inc(s, hv.base)
            dve.wait_ge(hz_ready, 2)
            with dve.Fori(0, HEADS) as h:
                b = lambda n: pv[:, bass.ds(h + (PAR_AT["b_mix"] + n * DT), 1)]
                own = lambda name: dve.wait_ge(s, hv.at(h, name))
                dve.wait_ge(ha.sem, ha.at(h, "sgq"))
                dve.scalar_tensor_tensor(hq, psum[:, 0, :], b(0), hq, ALU.add, ALU.mult).then_inc(s, 1)
                dve.wait_ge(ha.sem, ha.at(h, "sgg"))
                dve.scalar_tensor_tensor(hgl, psum[:, 1, :], b(3), hgl, ALU.add, ALU.mult).then_inc(s, 1)
                proj_done(dve, h, 3)
                dve.tensor_scalar(hz, psum[:, 2, :], b(1), None, ALU.add).then_inc(s, 1)
                proj_done(dve, h, 4)
                dve.tensor_copy(hv_tok, psum[:, 3, :]).then_inc(s, 1)
                dve.wait_ge(ha.sem, ha.at(h, "l1"))
                own("z")
                dve.scalar_tensor_tensor(hlf, hz, 0.0, hl1, ALU.min, ALU.subtract).then_inc(s, 1)
                own("lf")
                dve.scalar_tensor_tensor(hl1, hz, 0.0, hl1, ALU.max, ALU.add).then_inc(s, 1)
                own("t1")
                dve.tensor_scalar(hz, hz, -80.0, None, ALU.max).then_inc(s, 1)
                dve.wait_ge(ha.sem, ha.at(h, "l2"))
                dve.tensor_tensor(hlf, hlf, he1, ALU.add).then_inc(s, 1)
                dve.wait_ge(ha.sem, ha.at(h, "sn"))
                dve.tensor_scalar(hk, hk, lb[:, 1, bass.ds(h, 1)], None, ALU.mult).then_inc(s, 1)
                own("lf2")
                dve.tensor_tensor_scan(hB, chunk_start, hlf, 0.0, ALU.mult, ALU.add).then_inc(s, 1)
                own("B")
                B4 = hB.rearrange("p (c t) -> p c t", t=P)
                dve.tensor_tensor(hkd.rearrange("p (c t) -> p c t", t=P), B4[:, :, P - 1:P].to_broadcast([P, 4, P]), B4,
                                  ALU.subtract).then_inc(s, 1)
                for li, L in enumerate(LEVELS):
                    bl, br = halves(hB, L)
                    ol, o_r = halves(dl[:, li, :], L)
                    mid = bl[:, :, L - 1:L].to_broadcast([P, T // (2 * L), L])
                    dve.tensor_tensor(o_r, br, mid, ALU.subtract).then_inc(s, 1)
                    dve.tensor_tensor(ol, mid, bl, ALU.subtract).then_inc(s, 1)
                dve.wait_ge(ha.sem, ha.at(h, "EB"))
                dve.tensor_tensor(hqd, hq, hEB, ALU.mult).then_inc(s, 1)
                dve.wait_ge(ha.sem, ha.at(h, "Ekd"))
                dve.tensor_tensor(hkd, hkd, hk, ALU.mult).then_inc(s, 1)
                for li, L in enumerate(LEVELS):
                    dve.wait_ge(ha.sem, ha.at(h, "E0" if li < 4 else "E1"))
                    el, er = halves(dl[:, li, :], L)
                    dve.tensor_tensor(halves(ql[:, li, :], L)[1], halves(hq, L)[1], er, ALU.mult).then_inc(s, 1)
                    dve.tensor_tensor(halves(kl[:, li, :], L)[0], halves(hk, L)[0], el, ALU.mult).then_inc(s, 1)

                def scores(li):
                    dve.wait_ge(hi.sem, hi.at(h, f"s{li}"))
                    src = psum[:, 5 + li % 2, :].rearrange("p (c t) -> p c t", t=P)
                    dst = hsc.rearrange("p (c t) -> p c t", t=P)
                    if li == 0:
                        dve.tensor_copy(dst, src).then_inc(s, 1)
                    else:
                        own(f"c{li - 1}")
                        dve.memset(tick[:, :], 0.0)
                        m = same_block[:, li, :] if li < 7 else ident[:, :]
                        dve.copy_predicated(dst, m.bitcast(U32).unsqueeze(1).to_broadcast([P, 4, P]), src).then_inc(s, 1)

                scores(0)
                scores(1)
                dve.wait_ge(hi.sem, hi.at(h, "kv"))
                dve.tensor_copy(hst3[:, 0, :], psum[:, 7, 0:P]).then_inc(s, 1)
                for c in (1, 2):
                    own(f"S{c}")
                    dve.scalar_tensor_tensor(hst3[:, c, :], hst3[:, c - 1, :], hEB[:, c * P + P - 1:(c + 1) * P],
                                             psum[:, 7, c * P:(c + 1) * P], ALU.mult, ALU.add).then_inc(s, 1)
                for li in range(2, 8):
                    scores(li)
                dve.wait_ge(ha.sem, ha.at(h, "rstd"))
                dve.scalar_tensor_tensor(hl1, psum[:, 4, :], col("hg_norm"), hl1, ALU.mult, ALU.mult).then_inc(s, 1)
                own("y1")
                dve.tensor_tensor(y_hg[:, h, :], hl1, hgl, ALU.mult).then_inc(s, 1)

        lxp = work[:, 0:520]
        cup = work[:, 520:520 + 544]
        LU = lambda n: work[:, 1064 + n * T:1064 + (n + 1) * T]
        lsb, llg, lt1, lxb, lr, li_, la_t, lt_t, lw_t, lu_t = (LU(n) for n in range(10))
        gwt = work[:, 1064 + 10 * T:1064 + 10 * T + 256].rearrange("p (g j) -> p g j", g=2)
        lnsq = work[:, 8192:8192 + DT * T].rearrange("p (a t) -> p a t", t=T)
        mu = work[:, 12800:13312]
        lp = Steps(sem("lru_pe"), "r i", 2)
        la = Steps(sem("lru_act"), "lx sb lg sqg tg r i t a mult", 10)
        lv = Steps(sem("lru_dve"), "x0 x1 x2 x3 cu g1 g2 g3 " + " ".join(f"v{t}" for t in range(CONV))
                   + " ix den rden w u h yl")
        lv.base = len(lv.names)
        l_zero = sem("lru_zeros")
        gw_in = sem("gate_w_in")
        ln_pe = Steps(sem("ln_pe"), "mu var")
        ln_act = Steps(sem("ln_act"), " ".join(f"q{j}" for j in range(DT)) + " std " + " ".join(f"s{j}" for j in range(DT)))
        ln_dve = Steps(sem("ln_dve"), "mu " + " ".join(f"c{j}" for j in range(DT)) + " rstd "
                       + " ".join(f"n{j}" for j in range(DT)) + " " + " ".join(f"y{j}" for j in range(DT)))

        def lru_pool(pool):
            pool.wait_ge(hv.sem, hv.end(HEADS))
            pool.memset(lxp[:, 0:3], 0.0).then_inc(l_zero, 1)
            pool.memset(cup[:, 0:CONV - 1], 0.0).then_inc(l_zero, 1)
            with pool.Fori(0, DT) as j:
                pool.wait_ge(lp.sem, lp.at(j - 1, "i"))
                pool.dma_start(gwt, gate_w[:, j, :, :]).then_inc(gw_in, 16)

        def lru_proj(pe, j, j0, i):
            for bank, freed, who in ((0, "lx", la), (1, "lg", la), (2, "cu", lv), (3, "sb", la)):
                pe.wait_ge(who.sem, who.at(j - 1, freed))
                w = use_slab(pe, "lru", j0 + bank, i, 4)
                for k in range(DT):
                    ins = pe.matmul(psum[:, bank, :], w[:, k, :], xn[:, k, :], start=k == 0, stop=k == DT - 1)
                ins.then_inc(slab_used, 1)

        def lru_gates(pe, j):
            pe.wait_ge(lv.sem, lv.at(j, "x3"))
            pe.wait_ge(gw_in, j * 16 + 16)
            for g in range(2):
                pe.wait_ge(la.sem, la.at(j - 1, "ri"[g]))
                pe.matmul(psum[:, 4 + g, :], gwt[:, g, :], lxb, start=True, stop=True).then_inc(lp.sem, 1)

        def lru_pe(pe):
            pe.sem_inc(lp.sem, lp.base)
            pe.wait_ge(hv.sem, hv.end(HEADS))
            lru_proj(pe, 0, 0, 0)
            with pe.Fori(0, DT - 1) as j:
                lru_proj(pe, j + 1, 4, j)
                lru_gates(pe, j)
            lru_gates(pe, DT - 1)
            pe.wait_ge(lv.sem, lv.end(DT))
            for j in range(DT):
                ins = pe.matmul(psum[:, 6, :], ones[:, :], y_cv[:, j, :], start=j == 0, stop=j == DT - 1)
            ins.then_inc(ln_pe.sem, 1)
            for j in range(DT):
                pe.wait_ge(ln_act.sem, ln_act.at(0, f"q{j}"))
                ins = pe.matmul(psum[:, 7, :], ones[:, :], lnsq[:, j, :], start=j == 0, stop=j == DT - 1)
            ins.then_inc(ln_pe.sem, 1)

        def lru_act(act):
            s = la.sem
            act.sem_inc(s, la.base)
            act.wait_ge(l_zero, 2)
            with act.Fori(0, DT) as j:
                b = lambda n: pv[:, bass.ds(j + (PAR_AT["b_mix"] + n * DT), 1)]
                done = lambda n: act.wait_ge(slab_used, j * 4 + (SLAB_AT["lru"] + n))
                done(1)
                act.wait_ge(lv.sem, lv.at(j - 1, "x3"))
                act.activation(lxp[:, 3:3 + T], psum[:, 0, :], ACT.Identity, bias=b(4)).then_inc(s, 1)
                done(4)
                act.wait_ge(lv.sem, lv.at(j - 1, "cu"))
                act.activation(lsb, psum[:, 3, :], ACT.Sigmoid, bias=b(7)).then_inc(s, 1)
                act.wait_ge(lv.sem, lv.at(j - 1, "g3"))
                act.activation(llg, psum[:, 1, :], ACT.Identity, bias=b(5)).then_inc(s, 1)
                act.wait_ge(s, la.at(j, "lg"))
                act.wait_ge(lv.sem, lv.at(j - 1, "yl"))
                act.activation(lt1, llg, ACT.Square).then_inc(s, 1)
                act.wait_ge(lv.sem, lv.at(j, "g2"))
                act.activation(lt1, lt1, ACT.Tanh, scale=0.7978845608028654).then_inc(s, 1)
                for g in range(2):
                    act.wait_ge(lp.sem, lp.at(j, "ri"[g]))
                    act.activation((lr, li_)[g], psum[:, 4 + g, :], ACT.Sigmoid,
                                   bias=pv[:, bass.ds(j + (PAR_AT["gate_b"] + g * DT), 1)]).then_inc(s, 1)
                act.wait_ge(s, la.at(j, "r"))
                c = lru_c[:, bass.ds(j, 1)]
                act.activation(lt_t, lr, ACT.Tanh, scale=c).then_inc(s, 1)
                act.activation(la_t, lr, ACT.Exp, scale=c).then_inc(s, 1)
                act.wait_ge(lv.sem, lv.at(j, "w"))
                act.activation(lw_t, lw_t, ACT.Sqrt).then_inc(s, 1)
            s = ln_act.sem
            for j in range(DT):
                act.wait_ge(ln_dve.sem, ln_dve.at(0, f"c{j}"))
                act.activation(lnsq[:, j, :], y_cv[:, j, :], ACT.Square).then_inc(s, 1)
            act.wait_ge(ln_pe.sem, ln_pe.at(0, "var"))
            act.activation(std[:, :], psum[:, 7, :], ACT.Sqrt, bias=eps[:, 1:2], scale=1.0 / D).then_inc(s, 1)
            for j in range(DT):
                act.wait_ge(ln_dve.sem, ln_dve.at(0, f"n{j}"))
                act.activation(lnsq[:, j, :], y_cv[:, j, :], ACT.Sigmoid, bias=col("cv_ln_b", j)).then_inc(s, 1)

        def lru_dve(dve):
            s = lv.sem
            dve.sem_inc(s, lv.base)
            dve.wait_ge(l_zero, 2)
            with dve.Fori(0, DT) as j:
                own = lambda name: dve.wait_ge(s, lv.at(j, name))
                tap = lambda name, t: pv[:, bass.ds(j + (PAR_AT[name] + t * DT), 1)]
                dve.wait_ge(la.sem, la.at(j, "lx"))
                dve.tensor_scalar(lxb, lxp[:, 0:T], tap("lru_conv_w", 0), tap("lru_conv_b", 0), ALU.mult, ALU.add).then_inc(s, 1)
                for t in range(1, 4):
                    own(f"x{t - 1}")
                    dve.scalar_tensor_tensor(lxb, lxp[:, t:t + T], tap("lru_conv_w", t), lxb, ALU.mult, ALU.add).then_inc(s, 1)
                dve.wait_ge(la.sem, la.at(j, "sb"))
                dve.scalar_tensor_tensor(cup[:, CONV - 1:CONV - 1 + T], psum[:, 2, :], tap("b_mix", 6), lsb,
                                         ALU.add, ALU.mult).then_inc(s, 1)
                dve.wait_ge(la.sem, la.at(j, "sqg"))
                dve.tensor_scalar(lt1, lt1, 0.044715, 1.0, ALU.mult, ALU.add).then_inc(s, 1)
                own("g1")
                dve.tensor_tensor(lt1, lt1, llg, ALU.mult).then_inc(s, 1)
                dve.wait_ge(la.sem, la.at(j, "tg"))
                dve.scalar_tensor_tensor(lt1, lt1, 1.0, llg, ALU.add, ALU.mult).then_inc(s, 1)
                own("cu")
                acc = y_cv[:, j, :]
                dve.tensor_scalar(acc, cup[:, 0:T], tap("cv_w", 0), tap("cv_b", 0), ALU.mult, ALU.add).then_inc(s, 1)
                for t in range(1, CONV):
                    own(f"v{t - 1}")
                    dve.scalar_tensor_tensor(acc, cup[:, t:t + T], tap("cv_w", t), acc, ALU.mult, ALU.add).then_inc(s, 1)
                dve.wait_ge(la.sem, la.at(j, "i"))
                dve.tensor_tensor(li_, li_, lxb, ALU.mult).then_inc(s, 1)
                dve.wait_ge(la.sem, la.at(j, "t"))
                dve.tensor_scalar(lw_t, lt_t, -1.0, 1.0, ALU.mult, ALU.add).then_inc(s, 1)
                own("den")
                dve.reciprocal(lw_t, lw_t).then_inc(s, 1)
                own("rden")
                dve.scalar_tensor_tensor(lw_t, lt_t, -2.0, lw_t, ALU.mult, ALU.mult).then_inc(s, 1)
                dve.wait_ge(la.sem, la.at(j, "mult"))
                dve.tensor_tensor(lu_t, lw_t, li_, ALU.mult).then_inc(s, 1)
                own("u")
                dve.tensor_tensor_scan(lu_t, la_t, lu_t, 0.0, ALU.mult, ALU.add).then_inc(s, 1)
                own("h")
                dve.scalar_tensor_tensor(y_lru[:, j, :], lt1, 0.5, lu_t, ALU.mult, ALU.mult).then_inc(s, 1)
            s = ln_dve.sem
            dve.wait_ge(ln_pe.sem, ln_pe.at(0, "mu"))
            dve.tensor_scalar(mu, psum[:, 6, :], 1.0 / D, None, ALU.mult).then_inc(s, 1)
            dve.wait_ge(s, ln_dve.at(0, "mu"))
            for j in range(DT):
                dve.tensor_tensor(y_cv[:, j, :], y_cv[:, j, :], mu, ALU.subtract).then_inc(s, 1)
            dve.wait_ge(ln_act.sem, ln_act.at(0, "std"))
            dve.reciprocal(std[:, :], std[:, :]).then_inc(s, 1)
            dve.wait_ge(s, ln_dve.at(0, "rstd"))
            for j in range(DT):
                dve.scalar_tensor_tensor(y_cv[:, j, :], y_cv[:, j, :], col("cv_ln_g", j), std[:, :],
                                         ALU.mult, ALU.mult).then_inc(s, 1)
            for j in range(DT):
                dve.wait_ge(ln_act.sem, ln_act.at(0, f"s{j}"))
                dve.scalar_tensor_tensor(y_cv[:, j, :], y_cv[:, j, :], col("cv_ln_b", j), lnsq[:, j, :],
                                         ALU.add, ALU.mult).then_inc(s, 1)

        mg = work[:, 0:6 * T].rearrange("p (a t) -> p a t", t=T)
        ma = Steps(sem("merge_act"), "a b c", 3)
        md = Steps(sem("merge_dve"), "x y z xy out", 5)

        def merge_pe(pe):
            pe.wait_ge(ln_dve.sem, ln_dve.end(1))
            with pe.Fori(0, DT // 2) as i:
                for half in range(2):
                    m = 2 * i + half
                    for b in range(6):
                        if b < 3:
                            pe.wait_ge(ma.sem, ma.at(m - 1, "abc"[b]))
                        else:
                            pe.wait_ge(md.sem, md.at(m - 1, "xyz"[b - 3]))
                        w = use_slab(pe, "merge", 6 * half + b, i, 12)
                        src = (xn, xn, xn, y_hg, y_lru, y_cv)[b]
                        for k in range(DT):
                            ins = pe.matmul(psum[:, b, :], w[:, k, :], src[:, k, :], start=k == 0, stop=k == DT - 1)
                        ins.then_inc(slab_used, 1)
            pe.wait_ge(md.sem, md.end(DT))
            for m in range(DT):
                pe.wait_ge(resid_ready, DT + m - 1)
                w = use_slab(pe, "mix_out", m)
                for k in range(DT):
                    ins = pe.matmul(psum[:, 6 + m % 2, :], w[:, k, :], merged[:, k, :], start=k == 0, stop=k == DT - 1)
                ins.then_inc(slab_used, 1)

        def merge_act(act):
            act.sem_inc(ma.sem, ma.base)
            with act.Fori(0, DT) as m:
                for b in range(3):
                    act.wait_ge(slab_used, m * 6 + (SLAB_AT["merge"] + b + 1))
                    act.wait_ge(md.sem, md.at(m - 1, "xyz"[b]))
                    act.activation(mg[:, b, :], psum[:, b, :], ACT.Sigmoid,
                                   bias=pv[:, bass.ds(m + (PAR_AT["b_mix"] + (8 + b) * DT), 1)]).then_inc(ma.sem, 1)

        def merge_dve(dve):
            s = md.sem
            dve.sem_inc(s, md.base)
            with dve.Fori(0, DT) as m:
                dve.wait_ge(s, md.at(m - 1, "out"))
                for b in range(3):
                    dve.wait_ge(slab_used, m * 6 + (SLAB_AT["merge"] + b + 4))
                    dve.wait_ge(ma.sem, ma.at(m, "abc"[b]))
                    dst = mg[:, 3 + b, :]
                    dve.tensor_tensor(dst, mg[:, b, :], psum[:, 3 + b, :], ALU.mult).then_inc(s, 1)
                dve.wait_ge(s, md.at(m, "y"))
                dve.tensor_tensor(mg[:, 3, :], mg[:, 3, :], mg[:, 4, :], ALU.add).then_inc(s, 1)
                dve.wait_ge(s, md.at(m, "xy"))
                dve.tensor_tensor(merged[:, m, :], mg[:, 3, :], mg[:, 5, :], ALU.add).then_inc(s, 1)
            for m in range(DT):
                dve.wait_ge(slab_used, SLAB_AT["mix_out"] + m + 1)
                dve.tensor_tensor(resid[:, m, :], psum[:, 6 + m % 2, :], resid[:, m, :], ALU.add).then_inc(resid_ready, 1)

        Z = mem[:, 0:23 * TA].rearrange("p (n t) -> p n t", t=TA)
        vB = mem[:, 17664:17664 + 6 * T].rearrange("p (n c) -> p n c", c=T)
        hc = mem[:, 20736:20736 + DT * TC].rearrange("p (k t) -> p k t", t=TC)
        N0 = 22784
        sqc = mem[:, N0:N0 + DT * TC].rearrange("p (k t) -> p k t", t=TC)
        stdc = mem[:, N0 + DT * TC:N0 + DT * TC + TC]
        yb = mem[:, N0:N0 + 4 * T].rearrange("p (k t) -> p k t", t=T)
        mask = lambda n: shared[:, n * P:(n + 1) * P]
        same_head = mask(0)
        two_ident = shared[:, 17 * P:17 * P + 64]
        window = shared[:, 17 * P + 64:18 * P]
        cs = sb("cs", [P, 2 * DT])
        modv = sb("modv", [P, 48, 2])
        gm1 = sb("gm1", [P, DT, 2])
        gm2 = sb("gm2", [P, DT])
        mask_in = sem("mask_in")
        ctx_in = sem("ctx_in")
        cs_act = sem("cs_act")
        cs_dve = sem("cs_dve")
        mod_dve = sem("mod_dve")
        mid = sem("norm_mid")
        cn_act = Steps(sem("ctxnorm_act"), " ".join(f"q{j}" for j in range(DT)) + " std")
        cn_pe = sem("ctxnorm_pe")
        cn_dve = sem("ctxnorm_dve")
        in2_act = sem("in2_act")
        in2_dve = sem("in2_dve")
        v2_act = sem("v2_act")
        v2_dve = sem("v2_dve")
        spilled = sem("spilled")

        def mod_pe(pe):
            pe.wait_ge(resid_ready, 3 * DT)
            pe.wait_ge(cs_dve, 1)
            with pe.Fori(0, 12) as i:
                for j in range(4):
                    w = use_slab(pe, "mod", j, i, 4)
                    for k in range(DT):
                        ins = pe.matmul(psum[:, 6, bass.ds(i * 8 + 2 * j, 2)], w[:, k, :], cs[:, k:k + DT + 1:DT],
                                        start=k == 0, stop=k == DT - 1)
                    ins.then_inc(slab_used, 1)

        def mod_norm_dve(dve, n, gain, shift):
            dve.wait_ge(std_ready, n + 1)
            dve.reciprocal(std[:, :], std[:, :]).then_inc(rstd_ready, 1)
            dve.wait_ge(rstd_ready, n + 1)
            for j in range(DT):
                dve.scalar_tensor_tensor(xn[:, j, :], resid[:, j, :], gain(j), std[:, :], ALU.mult, ALU.mult).then_inc(mid, 1)
            for j in range(DT):
                dve.wait_ge(mid, DT * (n - 4) + j + 1)
                dve.tensor_scalar(xn[:, j, :], xn[:, j, :], shift(j), None, ALU.add).then_inc(xn_ready, 1)

        def block2_pool(pool):
            pool.wait_ge(resid_ready, 3 * DT)
            pool.dma_start(shared[:, 0:18 * P], masks).then_inc(mask_in, 16)
            pool.dma_start(hc, ctx_t).then_inc(ctx_in, 16)
            na_pool(pool)
            rwkv_pool(pool)
            merge2_pool(pool)
            moe_pool(pool)

        IN2 = [(0, 4, False), (4, 4, True), (8, 4, True), (12, 2, True), (14, 1, False), (15, 4, False), (19, 4, True)]

        def block2_pe(pe):
            norm_pe(pe, 4)
            for j in range(DT):
                pe.wait_ge(cn_act.sem, cn_act.at(0, f"q{j}"))
                ins = pe.matmul(psum[:, 5, 0:TC], ones[:, :], sqc[:, j, :], start=j == 0, stop=j == DT - 1)
            ins.then_inc(cn_pe, 1)
            pe.wait_ge(xn_ready, 5 * DT)
            pe.wait_ge(cn_dve, 1 + 2 * DT)
            u = 0
            for t0, n, both in IN2:
                for t in range(t0, t0 + n):
                    w = use_slab(pe, "in2", t)
                    if t >= 2:
                        pe.wait_ge(in2_act, t - 1)
                    for k in range(DT):
                        ins = pe.matmul(psum[:, t % 2, :], w[:, k, :], xn[:, k, :], start=k == 0, stop=k == DT - 1)
                    if both:
                        if u >= 2:
                            pe.wait_ge(in2_dve, u - 1)
                        for k in range(DT):
                            ins = pe.matmul(psum[:, 2 + u % 2, 0:TC], w[:, k, :], hc[:, k, :], start=k == 0, stop=k == DT - 1)
                        u += 1
                    ins.then_inc(slab_used, 1)
            pe.wait_ge(in2_act, 23)
            pe.wait_ge(in2_dve, 14)
            for s in range(4):
                w = use_slab(pe, "v2", s)
                for tt in range(6):
                    for kk in range(2):
                        k = 2 * s + kk
                        x = xn[:, k, tt * P:(tt + 1) * P] if tt < 4 else hc[:, k, (tt - 4) * P:(tt - 3) * P]
                        ins = pe.matmul(psum[:, tt, :], x, w[:, 4 * kk:4 * kk + 4, :], start=k == 0, stop=k == DT - 1,
                                        skip_group_check=True)
                ins.then_inc(slab_used, 1)
            na_pe(pe)
            rwkv_pe(pe)
            merge2_pe(pe)
            moe_pe(pe)

        def block2_act(act):
            norm_act(act, 4, 4 * DT, xn_ready)
            act.wait_ge(ctx_in, 16)
            for j in range(DT):
                act.activation(sqc[:, j, :], hc[:, j, :], ACT.Square).then_inc(cn_act.sem, 1)
            act.wait_ge(cn_pe, 1)
            act.activation(stdc, psum[:, 5, 0:TC], ACT.Sqrt, bias=eps[:, 0:1], scale=1.0 / D).then_inc(cn_act.sem, 1)
            act.wait_ge(xn_ready, 5 * DT)
            for t in range(23):
                act.wait_ge(slab_used, SLAB_AT["in2"] + t + 1)
                act.activation(Z[:, t, 0:T], psum[:, t % 2, :], ACT.Copy).then_inc(in2_act, 1)
            act.wait_ge(slab_used, SLAB_AT["v2"] + 4)
            for tt in range(3):
                act.activation(vB[:, tt, :], psum[:, tt, :], ACT.Copy).then_inc(v2_act, 1)
            na_act(act)
            rwkv_act(act)
            merge2_act(act)
            moe_act(act)

        def block2_dve(dve):
            dve.wait_ge(slab_used, SLAB_AT["mod"] + 48)
            dve.tensor_tensor(modv[:, :, :], psum[:, 6, 0:96].rearrange("p (m s) -> p m s", s=2),
                              col("mod_b", 0, 48).unsqueeze(2).to_broadcast([P, 48, 2]), ALU.add).then_inc(mod_dve, 1)
            dve.wait_ge(mod_dve, 1)
            dve.scalar_tensor_tensor(gm1[:, :, :], modv[:, DT:2 * DT, :], 1.0,
                                     col("norm1", 0, DT).unsqueeze(2).to_broadcast([P, DT, 2]), ALU.add, ALU.mult).then_inc(mod_dve, 1)
            dve.scalar_tensor_tensor(gm2[:, :], modv[:, 4 * DT:5 * DT, 0], 1.0, col("norm2", 0, DT), ALU.add, ALU.mult).then_inc(mod_dve, 1)
            dve.wait_ge(mod_dve, 3)
            mod_norm_dve(dve, 4, lambda j: gm1[:, j, 0:1], lambda j: modv[:, j, 0:1])
            dve.wait_ge(cn_act.sem, cn_act.at(0, "std"))
            dve.reciprocal(stdc, stdc).then_inc(cn_dve, 1)
            dve.wait_ge(cn_dve, 1)
            for j in range(DT):
                dve.scalar_tensor_tensor(hc[:, j, :], hc[:, j, :], gm1[:, j, 1:2], stdc, ALU.mult, ALU.mult).then_inc(cn_dve, 1)
            for j in range(DT):
                dve.wait_ge(cn_dve, 2 + j)
                dve.tensor_scalar(hc[:, j, :], hc[:, j, :], modv[:, j, 1:2], None, ALU.add).then_inc(cn_dve, 1)
            u = 0
            for t0, n, both in IN2:
                for t in range(t0, t0 + n):
                    if both:
                        dve.wait_ge(slab_used, SLAB_AT["in2"] + t + 1)
                        dve.tensor_copy(Z[:, t, T:TA], psum[:, 2 + u % 2, 0:TC]).then_inc(in2_dve, 1)
                        u += 1
            dve.wait_ge(slab_used, SLAB_AT["v2"] + 4)
            for tt in range(3, 6):
                dve.tensor_copy(vB[:, tt, :], psum[:, tt, :]).then_inc(v2_dve, 1)
            na_dve(dve)
            rwkv_dve(dve)
            merge2_dve(dve)
            moe_dve(dve)

        A0 = N0 + 4 * T
        qn = mem[:, A0:A0 + T]
        kn = mem[:, A0 + T:A0 + T + TA]
        tq = mem[:, A0 + 1280:A0 + 1280 + TA]
        sc = mem[:, A0 + 2048:A0 + 2048 + 2 * TA].rearrange("p (b k) -> p b k", b=2)
        pT = mem[:, A0 + 3584:A0 + 3584 + 2 * TA].rearrange("p (b k) -> p b k", b=2)
        rb = mem[:, A0 + 5120:A0 + 5120 + 2048].rearrange("p (h j c) -> p h j c", h=2, j=16)
        osb = mem[:, A0 + 7168:A0 + 7168 + T].rearrange("p (q c) -> p q c", q=4)
        tqq = mem[:, A0 + 7680:A0 + 7680 + T]
        stat = mem[:, A0 + 8192:A0 + 8192 + 32].rearrange("p (s u) -> p s u", s=4)
        U8 = range(8)
        na = Steps(sem("na_act"), "sqq sqk rq rk rkc e0 " + " ".join(f"e{u + 1} t{u}" for u in range(7)) + " t7 y", 22)
        nd = Steps(sem("na_dve"), "iq ik qn kn a0 b0 m0 n0 " + " ".join(f"a{u + 1} b{u + 1} m{u + 1} n{u + 1} d{u} i{u} o{u}" for u in range(7))
                   + " d7 i7 o7")
        nd.base = len(nd.names)
        assert na.base == len(na.names)
        npe = Steps(sem("na_pe"), "nq nk s0 " + " ".join(f"s{u + 1} t{u} o{u}" for u in range(7)) + " t7 o7 y", 28)
        npe.base = len(npe.names)
        rb_in = sem("rb_in")
        rb_pool = sem("rb_pool")

        def na_pool(pool):
            pool.wait_ge(mask_in, 16)
            pool.wait_ge(cn_dve, 1 + 2 * DT)
            with pool.Fori(0, 4) as p:
                pool.wait_ge(nd.sem, nd.at(p - 1, "a7"))
                for hh in range(2):
                    pool.dma_start(rb[:, hh, :, :], rpb[2 * p + hh].rearrange("p (j c) -> p j c", j=16)).then_inc(rb_in, 16)
                pool.wait_ge(rb_in, p * 32 + 32)
                for hh in range(2):
                    pool.tensor_tensor(rb[:, hh, :, :], rb[:, hh, :, :], window.unsqueeze(1).to_broadcast([P, 16, 64]),
                                       ALU.add).then_inc(rb_pool, 1)

        def na_pe(pe):
            pe.sem_inc(npe.sem, npe.base)
            pe.wait_ge(mask_in, 16)
            pe.wait_ge(v2_act, 3)
            pe.wait_ge(v2_dve, 3)
            with pe.Fori(0, 4) as p:
                s = npe.sem
                pe.wait_ge(na.sem, na.at(p, "sqq"))
                pe.wait_ge(na.sem, na.at(p - 1, "t7"))
                pe.matmul(psum[:, 4, :], same_head, tqq, start=True, stop=True).then_inc(s, 1)
                pe.wait_ge(na.sem, na.at(p, "sqk"))
                pe.wait_ge(nd.sem, nd.at(p - 1, "o7"))
                pe.matmul(psum[:, 5, :], same_head, tq[:, 0:T], start=True, stop=True)
                pe.matmul(psum[:, 6, 0:TC], same_head, tq[:, T:TA], start=True, stop=True).then_inc(s, 1)

                def scores(u):
                    hh, qt = u // 4, u % 4
                    r = slice(64 * hh, 64 * hh + 64)
                    if u >= 2:
                        pe.wait_ge(nd.sem, nd.at(p, f"b{u - 2}"))
                    else:
                        pe.wait_ge(nd.sem, nd.at(p, "kn"))
                    pe.matmul(psum[:, u % 2, :], qn[r, qt * P:(qt + 1) * P], kn[r, 0:T], start=True, stop=True)
                    pe.matmul(psum[:, 2 + u % 2, 0:TC], qn[r, qt * P:(qt + 1) * P], kn[r, T:TA], start=True, stop=True).then_inc(s, 1)

                def values(u):
                    hh = u // 4
                    pe.wait_ge(na.sem, na.at(p, f"e{u}"))
                    if u:
                        pe.wait_ge(na.sem, na.at(p, f"t{u - 1}"))
                        pe.wait_ge(nd.sem, nd.at(p, f"o{u - 1}"))
                    else:
                        pe.wait_ge(na.sem, na.at(p, "rkc"))
                    for kt in range(6):
                        ins = pe.transpose(psum[:, 4 + kt // 4, (kt % 4) * P:(kt % 4 + 1) * P], sc[:, u % 2, kt * P:(kt + 1) * P],
                                           ident[:, :])
                    ins.then_inc(s, 1)
                    pe.wait_ge(na.sem, na.at(p, f"t{u}"))
                    pe.wait_ge(nd.sem, nd.at(p, f"d{u}"))
                    for kt in range(6):
                        ins = pe.matmul(psum[:, 6, 0:64], pT[:, u % 2, kt * P:(kt + 1) * P],
                                        vB[:, kt, bass.ds(p * P + 64 * hh, 64)], start=kt == 0, stop=kt == 5)
                    ins.then_inc(s, 1)

                scores(0)
                for u in U8:
                    if u < 7:
                        scores(u + 1)
                    values(u)
                pe.wait_ge(nd.sem, nd.at(p, "o7"))
                pe.wait_ge(na.sem, na.at(p - 1, "y"))
                for qt in range(4):
                    ins = pe.transpose(psum[:, 7, qt * P:(qt + 1) * P], osb[:, qt, :], ident[:, :])
                ins.then_inc(s, 1)

        def na_act(act):
            s = na.sem
            act.sem_inc(s, na.base)
            act.wait_ge(in2_dve, 14)
            act.wait_ge(cn_dve, 1 + 2 * DT)
            with act.Fori(0, 4) as p:
                act.wait_ge(nd.sem, nd.at(p - 1, "kn"))
                act.activation(tqq, Z[:, bass.ds(p + 15, 1), 0:T].rearrange("p a t -> p (a t)"), ACT.Square).then_inc(s, 1)
                act.activation(tq, Z[:, bass.ds(p + 19, 1), :].rearrange("p a t -> p (a t)"), ACT.Square).then_inc(s, 1)
                act.wait_ge(npe.sem, npe.at(p, "nq"))
                act.activation(tqq, psum[:, 4, :], ACT.Sqrt, bias=eps[:, 3:4], scale=1.0).then_inc(s, 1)
                act.wait_ge(npe.sem, npe.at(p, "nk"))
                act.activation(tq[:, 0:T], psum[:, 5, :], ACT.Sqrt, bias=eps[:, 0:1], scale=1.0 / 64).then_inc(s, 1)
                act.activation(tq[:, T:TA], psum[:, 6, 0:TC], ACT.Sqrt, bias=eps[:, 0:1], scale=1.0 / 64).then_inc(s, 1)

                def probs(u):
                    act.wait_ge(nd.sem, nd.at(p, f"n{u}"))
                    act.activation(sc[:, u % 2, :], sc[:, u % 2, :], ACT.Exp, bias=stat[:, 1, u:u + 1],
                                   accum_out=stat[:, 2, u:u + 1]).then_inc(s, 1)

                probs(0)
                for u in U8:
                    if u < 7:
                        probs(u + 1)
                    act.wait_ge(npe.sem, npe.at(p, f"t{u}"))
                    act.activation(pT[:, u % 2, 0:T], psum[:, 4, :], ACT.Copy).then_inc(s, 1)
                act.wait_ge(npe.sem, npe.at(p, "y"))
                act.activation(yb[:, bass.ds(p, 1), :].rearrange("p a t -> p (a t)"), psum[:, 7, :], ACT.Copy).then_inc(s, 1)

        def na_dve(dve):
            s = nd.sem
            dve.sem_inc(s, nd.base)
            dve.wait_ge(in2_act, 23)
            with dve.Fori(0, 4) as p:
                own = lambda name: dve.wait_ge(s, nd.at(p, name))
                dve.wait_ge(na.sem, na.at(p, "rq"))
                dve.reciprocal(tqq, tqq).then_inc(s, 1)
                dve.wait_ge(na.sem, na.at(p, "rkc"))
                dve.reciprocal(tq, tq).then_inc(s, 1)
                own("iq")
                dve.wait_ge(npe.sem, npe.at(p - 1, "o7"))
                dve.scalar_tensor_tensor(qn, Z[:, bass.ds(p + 15, 1), 0:T].rearrange("p a t -> p (a t)"), col("q_g"), tqq,
                                         ALU.mult, ALU.mult).then_inc(s, 1)
                own("ik")
                dve.scalar_tensor_tensor(kn, Z[:, bass.ds(p + 19, 1), :].rearrange("p a t -> p (a t)"), col("k_g"), tq,
                                         ALU.mult, ALU.mult).then_inc(s, 1)

                def logits(u):
                    hh, qt = u // 4, u % 4
                    dve.wait_ge(npe.sem, npe.at(p, f"s{u}"))
                    if u >= 2:
                        dve.wait_ge(npe.sem, npe.at(p, f"t{u - 2}"))
                    if u == 0:
                        dve.wait_ge(rb_pool, p * 2 + 2)
                    dve.tensor_tensor(sc[:, u % 2, 0:T].rearrange("p (j c) -> p j c", j=8), psum[:, u % 2, :].rearrange("p (j c) -> p j c", j=8),
                                      rb[:, hh, 7 - 2 * qt:15 - 2 * qt, :], ALU.add).then_inc(s, 1)
                    dve.tensor_copy(sc[:, u % 2, T:TA], psum[:, 2 + u % 2, 0:TC]).then_inc(s, 1)
                    own(f"b{u}")
                    dve.tensor_reduce(stat[:, 0, u:u + 1], sc[:, u % 2, :], AX.X, ALU.max).then_inc(s, 1)
                    own(f"m{u}")
                    dve.tensor_scalar(stat[:, 1, u:u + 1], stat[:, 0, u:u + 1], -1.0, None, ALU.mult).then_inc(s, 1)

                logits(0)
                for u in U8:
                    hh, qt = u // 4, u % 4
                    if u < 7:
                        logits(u + 1)
                    dve.wait_ge(npe.sem, npe.at(p, f"t{u}"))
                    dve.tensor_copy(pT[:, u % 2, T:TA], psum[:, 5, 0:TC]).then_inc(s, 1)
                    dve.wait_ge(na.sem, na.at(p, f"e{u}"))
                    dve.reciprocal(stat[:, 3, u:u + 1], stat[:, 2, u:u + 1]).then_inc(s, 1)
                    own(f"i{u}")
                    dve.wait_ge(npe.sem, npe.at(p, f"o{u}"))
                    if u == 0:
                        dve.wait_ge(npe.sem, npe.at(p - 1, "y"))
                    dve.tensor_scalar(osb[:, qt, 64 * hh:64 * hh + 64], psum[:, 6, 0:64], stat[:, 3, u:u + 1], None,
                                      ALU.mult).then_inc(s, 1)

        C0 = 0.6065306597126334
        L = 64
        regions = {"a": [15 * TA, N0], "b": [N0 + 4 * T, 69 * T]}

        def take(n, where):
            lo, hi_ = regions[where]
            assert lo + n <= hi_, (where, n)
            regions[where][0] += n
            return mem[:, lo:lo + n]

        bd = lambda v: v.rearrange("p (q t) -> p q t", q=4)
        dirs = []
        for d in range(2):
            w = "ab"[d]
            names = "kap bt kt rho v kT bT AT CT R1 R2 X XT Ym".split()
            g = {n: bd(take(4 * P, w)) for n in names}
            g.update({n: bd(take(4 * L, w)) for n in ("vt", "G", "Un", "st")})
            dirs.append(g)
        res_f = resid[:, :, :].rearrange("p a t -> p (a t)")
        kkn = res_f[:, 0:4 * TA].rearrange("p (q t) -> p q t", q=4)
        sgb = res_f[:, 3072:3584]
        csb, exb = res_f[:, 3584:3840], res_f[:, 3840:4096]
        yacc = take(8 * 4 * L, "a").rearrange("p (c q v) -> p c q v", c=8, q=4)
        pinc, pexc, pinv, tb, tk = (take(4 * L, "b") for _ in range(5))
        reset = take(4 * L, "a")
        lw_c = [take(2 * L, "b") for _ in range(2)]
        wab = take(16, "a").rearrange("p (d n) -> p d n", d=2)
        plast = [take(4, "a") for _ in range(2)]
        wlo = [take(T, "a"), take(T, "b")]
        wg = Z[:, 0:2, T:TA]
        knt = mem[:, 15 * TA:15 * TA + 4 * TA].rearrange("p (q t) -> p q t", q=4)
        ya = mem[:, 15 * TA:15 * TA + 4 * T].rearrange("p (q t) -> p q t", q=4)

        LV = range(1, 6)

        def steps_of(tag, emit):
            e = lambda s: s if emit else ""
            both = lambda f: " ".join(f(d) for d in range(2))
            act_n = both(lambda d: f"lw{d} la{d} th{d} pi{d} pv{d} pe{d}") + " " + both(lambda d: f"AT{d} kT{d} bT{d} vt{d}") \
                + " un0 un1"
            dve_n = both(lambda d: f"t{d} sg{d} cs{d} ex{d} b{d} ka{d} kd{d} bh{d}0 bh{d}1 kh{d}0 kh{d}1 pl{d}") + " " \
                + both(lambda d: f"m{d} x0{d} n{d} xt0{d} CT{d} " + e(f"R1{d} R2{d}")) + " " \
                + " ".join(both(lambda d: f"ym{l}{d}") + " " + both(lambda d: (f"x{l}{d} " if l < 5 else "") + f"xt{l}{d}") for l in LV) \
                + " g0 g1 " + both(lambda d: f"z{d} zz{d} " + e(f"y{d}"))
            pool_n = both(lambda d: f"v{d}0 v{d}1 kp{d}0 kp{d}1 " + e(f"r{d}0 r{d}1"))
            pe_n = "wa0 wa1 " + both(lambda d: f"AT{d} A{d} CT{d} " + e(f"R1{d} R2{d} ") + f"kT{d} bT{d} vt{d}") + " " \
                + " ".join(both(lambda d: f"Y{l}{d}") + " " + both(lambda d: (f"XY{l}{d} " if l < 5 else "") + f"YX{l}{d}") for l in LV) \
                + " G0 G1 U0 U1 " + both(lambda d: f"Z{d} " + e(f"y{d}"))
            out = []
            for who, names in (("act", act_n), ("dve", dve_n), ("pool", pool_n), ("pe", pe_n)):
                s = Steps(sem(f"rwkv_{tag}_{who}"), names)
                s.base = len(s.names)
                out.append(s)
            return out

        RS = {False: steps_of("ctx", False), True: steps_of("lat", True)}
        kn_act = Steps(sem("keynorm_act"), "s0 s1 s2 s3 r0 r1 r2 r3")
        kn_dve = Steps(sem("keynorm_dve"), "k0 k1 k2 k3 m0 m1 m2 m3 n0 n1 n2 n3 i0 i1 i2 i3 f0 f1 f2 f3 w0 w1 w2 w3")
        kn_pe = sem("keynorm_pe")
        rz = sem("rwkv_zeros")
        lora_in = sem("lora_in")

        def first_token(c, d, emit):
            if emit:
                return c * L if d == 0 else c * -L + (T - L)
            return c * L + T if d == 0 else c * -L + (TA - L)

        def seq(base, c, d, emit, rows=slice(None)):
            o = first_token(c, d, emit)
            src = kkn if base is None else Z[:, base:base + 4, :]
            return src[rows, :, bass.ds(o, L)]

        def rwkv_pool(pool):
            pool.wait_ge(xn_ready, 5 * DT)
            pool.dma_start(spill, resid[:, :, :]).then_inc(spilled, 16)
            pool.wait_ge(na.sem, na.end(4))
            pool.dma_start(wlo[0], lora[:, 0, :]).then_inc(lora_in, 16)
            pool.dma_start(wlo[1], lora[:, 1, :]).then_inc(lora_in, 16)
            pool.dma_start(wg, lora[:, 2, :].rearrange("p (a c) -> p a c", a=2)).then_inc(lora_in, 16)
            pool.wait_ge(kn_dve.sem, kn_dve.end(1))
            for d in range(2):
                for n in "kap bt kt rho v st".split():
                    pool.memset(dirs[d][n], 0.0).then_inc(rz, 1)
            pool.memset(yacc, 0.0).then_inc(rz, 1)
            pool.memset(reset, 1.0).then_inc(rz, 1)
            pool.wait_ge(rz, 14)
            pool.memset(reset.rearrange("p (q t) -> p q t", q=4)[:, :, 0:1], 0.0).then_inc(rz, 1)
            pool.wait_ge(rz, 15)
            for emit in (False, True):
                ra, rd, rp, re = RS[emit]
                if emit:
                    pool.wait_ge(RS[False][3].sem, RS[False][3].end(4))
                pool.sem_inc(rp.sem, rp.base)
                with pool.Fori(0, 8 if emit else 4) as c:
                    for d in range(2):
                        g = dirs[d]
                        H = [(slice(0, 64), slice(0, 64)), (slice(64, 128), slice(64, 128))]
                        pool.wait_ge(re.sem, re.at(c - 1, f"vt{d}"))
                        for r, k in H:
                            pool.tensor_copy(g["v"][r, :, k], seq(8, c, d, emit, r)).then_inc(rp.sem, 1)
                        pool.wait_ge(ra.sem, ra.at(c, f"pe{d}"))
                        pool.wait_ge(re.sem, re.at(c - 1, f"G{d}"))
                        for r, k in H:
                            pool.tensor_tensor(g["kap"][r, :, k], seq(None, c, d, emit, r), bd(pexc)[r], ALU.mult).then_inc(rp.sem, 1)
                        if emit:
                            pool.wait_ge(re.sem, re.at(c - 1, f"y{d}"))
                            for r, k in H:
                                pool.tensor_tensor(g["rho"][r, :, k], seq(0, c, d, emit, r), bd(pinc)[r], ALU.mult).then_inc(rp.sem, 1)

            rwkv_out_pool(pool)

        def rwkv_act(act):
            s = kn_act.sem
            for t in range(4):
                act.wait_ge(kn_dve.sem, kn_dve.at(0, f"k{t}"))
                act.activation(knt[:, t, :], kkn[:, t, :], ACT.Square).then_inc(s, 1)
            for t in range(4):
                act.wait_ge(kn_dve.sem, kn_dve.at(0, f"n{t}"))
                act.activation(knt[:, t, :], knt[:, t, :], ACT.Sqrt).then_inc(s, 1)
            for emit in (False, True):
                ra, rd, rp, re = RS[emit]
                s = ra.sem
                if emit:
                    for o in RS[False][1:]:
                        act.wait_ge(o.sem, o.end(4))
                else:
                    act.wait_ge(kn_dve.sem, kn_dve.end(1))
                act.sem_inc(s, ra.base)
                with act.Fori(0, 8 if emit else 4) as c:
                    for d in range(2):
                        o = first_token(c, d, emit)
                        act.wait_ge(re.sem, re.at(c - 1, f"wa{d}"))
                        act.activation(lw_c[d][:, 0:L], Z[:, 12, bass.ds(o, L)], ACT.Tanh).then_inc(s, 1)
                        act.activation(lw_c[d][:, L:2 * L], Z[:, 13, bass.ds(o, L)], ACT.Copy).then_inc(s, 1)
                        act.wait_ge(rd.sem, rd.at(c, f"t{d}"))
                        act.activation(sgb, sgb, ACT.Tanh, scale=0.5).then_inc(s, 1)
                        act.wait_ge(rd.sem, rd.at(c, f"cs{d}"))
                        pc, pd = (c, 0) if d else (c - 1, 1)
                        act.wait_ge(rd.sem, rd.at(pc, f"pl{pd}"))
                        act.wait_ge(rp.sem, rp.at(pc, f"r{pd}1" if emit else f"kp{pd}1"))
                        act.activation(pinc, csb, ACT.Exp, scale=-C0).then_inc(s, 1)
                        act.activation(pinv, csb, ACT.Exp, scale=C0).then_inc(s, 1)
                        act.wait_ge(rd.sem, rd.at(c, f"ex{d}"))
                        act.activation(pexc, exb, ACT.Exp, scale=-C0).then_inc(s, 1)
                    for d in range(2):
                        g, B = dirs[d], 4 * d
                        for name, bank, dst in (("AT", B, g["AT"]), ("kT", B + 1, g["kT"]), ("bT", B + 2, g["bT"])):
                            act.wait_ge(re.sem, re.at(c, f"{name}{d}"))
                            act.activation(dst, psum[:, bank, :].rearrange("p (q t) -> p q t", q=4), ACT.Copy).then_inc(s, 1)
                        act.wait_ge(re.sem, re.at(c, f"vt{d}"))
                        act.activation(g["vt"], bd(psum[:, B + 3, 0:4 * L]), ACT.Copy).then_inc(s, 1)
                    for d in range(2):
                        act.wait_ge(re.sem, re.at(c, f"U{d}"))
                        act.activation(dirs[d]["Un"], bd(psum[:, 4 * d + 3, 4 * L:8 * L]), ACT.Copy, scale=-1.0).then_inc(s, 1)
            rwkv_out_act(act)

        def rwkv_pe(pe):
            for t in range(4):
                pe.wait_ge(kn_act.sem, kn_act.at(0, f"s{t}"))
                if t == 0:
                    pe.wait_ge(na.sem, na.end(4))
                    pe.wait_ge(nd.sem, nd.end(4))
                pe.matmul(psum[:, 2 * t, :], same_head, knt[:, t, 0:T], start=True, stop=True)
                pe.matmul(psum[:, 2 * t + 1, 0:TC], same_head, knt[:, t, T:TA], start=True, stop=True).then_inc(kn_pe, 1)
            pe.wait_ge(lora_in, 48)
            pe.wait_ge(rz, 15)
            pe.wait_ge(kn_dve.sem, kn_dve.end(1))
            for emit in (False, True):
                ra, rd, rp, re = RS[emit]
                s = re.sem
                if emit:
                    pe.wait_ge(RS[False][1].sem, RS[False][1].end(4))
                    pe.wait_ge(RS[False][0].sem, RS[False][0].end(4))
                pe.sem_inc(s, re.base)
                with pe.Fori(0, 8 if emit else 4) as c:
                    W = lambda st, name, u=c: pe.wait_ge(st.sem, st.at(u, name))
                    Q = range(4)

                    def prod(name, bank, lhs, rhs, n=P):
                        for q in Q:
                            ins = pe.matmul(psum[:, bank, q * n:(q + 1) * n], lhs[:, q, :], rhs if rhs is two_ident else rhs[:, q, :],
                                            start=True, stop=True)
                        ins.then_inc(s, 1)

                    for d in range(2):
                        W(ra, f"la{d}")
                        W(rd, f"zz{d}", c - 1)
                        rows = slice(64 * d, 64 * d + 64)
                        for m in range(2):
                            for q in Q:
                                ins = pe.matmul(psum[:, 4 * d, (4 * m + q) * L:(4 * m + q + 1) * L],
                                                wlo[m][rows, q * P:(q + 1) * P],
                                                lw_c[d][rows, m * L:(m + 1) * L], start=True, stop=True)
                        ins.then_inc(s, 1)
                    for d in range(2):
                        g, B = dirs[d], 4 * d
                        W(rd, f"bh{d}1")
                        W(rp, f"kp{d}1")
                        prod("AT", B, g["bt"], g["kap"])
                        if emit:
                            W(rd, f"y{d}", c - 1)
                        prod("A", B + 1, g["kap"], g["bt"])
                        W(rd, f"kh{d}1")
                        prod("CT", B + 2, g["kt"], g["kap"])
                        if emit:
                            W(rp, f"r{d}1")
                            prod("R1", B + 3, g["kt"], g["rho"])
                            W(ra, f"AT{d}")
                            prod("R2", B, g["bt"], g["rho"])
                        W(rd, f"m{d}")
                        for name, bank, src in (("kT", B + 1, g["kt"]), ("bT", B + 2, g["bt"])):
                            if name == "bT":
                                W(rd, f"CT{d}")
                            for q in Q:
                                ins = pe.transpose(psum[:, bank, q * P:(q + 1) * P], src[:, q, :], ident[:, :])
                            ins.then_inc(s, 1)
                        if emit:
                            W(rd, f"R1{d}")
                        W(rp, f"v{d}1")
                        prod("vt", B + 3, g["v"], two_ident, L)
                    for l in LV:
                        for d in range(2):
                            g, B = dirs[d], 4 * d
                            W(rd, f"x{l - 1}{d}")
                            if l == 1:
                                W(ra, f"AT{d}")
                                if emit:
                                    W(rd, f"R2{d}")
                            prod("Y", B, g["AT"], g["X"])
                        for d in range(2):
                            g, B = dirs[d], 4 * d
                            W(rd, f"ym{l}{d}")
                            W(rd, f"xt{l - 1}{d}")
                            if l == 1:
                                W(ra, f"bT{d}")
                            if l < 5:
                                prod("XY", B + 1, g["XT"], g["Ym"])
                            prod("YX", B + 2, g["Ym"], g["XT"])
                    for d in range(2):
                        g, B = dirs[d], 4 * d
                        W(ra, f"vt{d}")
                        for q in Q:
                            pe.matmul(psum[:, B + 3, q * L:(q + 1) * L], g["kap"][:, q, :], g["st"][:, q, :], start=True, stop=False)
                            ins = pe.matmul(psum[:, B + 3, q * L:(q + 1) * L], g["CT"][:, q, :], g["vt"][:, q, :], start=False, stop=True)
                        ins.then_inc(s, 1)
                    for d in range(2):
                        g, B = dirs[d], 4 * d
                        W(rd, f"g{d}")
                        W(rd, f"xt5{d}")
                        for q in Q:
                            ins = pe.matmul(psum[:, B + 3, (4 + q) * L:(5 + q) * L], g["XT"][:, q, :], g["G"][:, q, :], start=True, stop=True)
                        ins.then_inc(s, 1)
                    for d in range(2):
                        g, B = dirs[d], 4 * d
                        W(ra, f"un{d}")
                        for q in Q:
                            o = psum[:, B, q * L:(q + 1) * L]
                            pe.matmul(o, g["kT"][:, q, :], g["vt"][:, q, :], start=True, stop=False)
                            ins = pe.matmul(o, g["bT"][:, q, :], g["Un"][:, q, :], start=False, stop=True)
                        ins.then_inc(s, 1)
                        if emit:
                            for q in Q:
                                o = psum[:, B + 1, q * L:(q + 1) * L]
                                pe.matmul(o, g["rho"][:, q, :], g["st"][:, q, :], start=True, stop=False)
                                pe.matmul(o, g["R1"][:, q, :], g["vt"][:, q, :], start=False, stop=False)
                                ins = pe.matmul(o, g["R2"][:, q, :], g["Un"][:, q, :], start=False, stop=True)
                            ins.then_inc(s, 1)
            rwkv_out_pe(pe)

        def rwkv_dve(dve):
            s = kn_dve.sem
            W = lambda n: dve.wait_ge(s, kn_dve.at(0, n))
            dve.wait_ge(spilled, 16)
            dve.wait_ge(na.sem, na.end(4))
            dve.wait_ge(npe.sem, npe.end(4))
            for t in range(4):
                dve.tensor_scalar(kkn[:, t, :], Z[:, 4 + t, :], col("k_k", t), None, ALU.mult).then_inc(s, 1)
            for t in range(4):
                dve.wait_ge(kn_pe, t + 1)
                dve.tensor_scalar(knt[:, t, 0:T], psum[:, 2 * t, :], 1e-12, None, ALU.max).then_inc(s, 1)
            for t in range(4):
                dve.tensor_scalar(knt[:, t, T:TA], psum[:, 2 * t + 1, 0:TC], 1e-12, None, ALU.max).then_inc(s, 1)
            for t in range(4):
                dve.wait_ge(kn_act.sem, kn_act.at(0, f"r{t}"))
                dve.reciprocal(knt[:, t, :], knt[:, t, :]).then_inc(s, 1)
            for t in range(4):
                W(f"i{t}")
                dve.tensor_tensor(kkn[:, t, :], kkn[:, t, :], knt[:, t, :], ALU.mult).then_inc(s, 1)
            for d in range(2):
                dve.tensor_copy(wab[:, d, 0:4], col("w0", 4 * d, 4)).then_inc(s, 1)
                dve.tensor_copy(wab[:, d, 4:8], col("a0", 4 * d, 4)).then_inc(s, 1)
            W("w3")
            dve.wait_ge(rz, 15)
            H = [(slice(0, 64), slice(0, 64)), (slice(64, 128), slice(64, 128))]
            I4 = ident[:, :].unsqueeze(1).to_broadcast([P, 4, P])
            m4 = lambda n: mask(n).unsqueeze(1).to_broadcast([P, 4, P])
            P4 = lambda b: psum[:, b, :].rearrange("p (q t) -> p q t", q=4)
            for emit in (False, True):
                ra, rd, rp, re = RS[emit]
                s = rd.sem
                if emit:
                    dve.wait_ge(RS[False][3].sem, RS[False][3].end(4))
                    dve.wait_ge(RS[False][2].sem, RS[False][2].end(4))
                dve.sem_inc(s, rd.base)
                with dve.Fori(0, 8 if emit else 4) as c:
                    own = lambda name, u=c: dve.wait_ge(s, rd.at(u, name))
                    A = lambda name, u=c: dve.wait_ge(ra.sem, ra.at(u, name))
                    E_ = lambda name, u=c: dve.wait_ge(re.sem, re.at(u, name))
                    for d in range(2):
                        g = dirs[d]
                        own("kh01" if d else "kh11", c if d else c - 1)
                        E_(f"wa{d}")
                        dve.tensor_tensor(sgb.rearrange("p (n t) -> p n t", n=8), psum[:, 4 * d, :].rearrange("p (n t) -> p n t", n=8),
                                          wab[:, d, :].unsqueeze(2).to_broadcast([P, 8, L]), ALU.add).then_inc(s, 1)
                        A(f"th{d}")
                        dve.tensor_scalar(sgb, sgb, 0.5, 0.5, ALU.mult, ALU.add).then_inc(s, 1)
                        own(f"sg{d}")
                        sw, a = sgb[:, 0:4 * L], bd(sgb[:, 4 * L:8 * L])
                        if d:
                            dve.tensor_tensor_scan(csb[:, ::-1], reset, sw[:, ::-1], 0.0, ALU.mult, ALU.add).then_inc(s, 1)
                        else:
                            dve.tensor_tensor_scan(csb, reset, sw, 0.0, ALU.mult, ALU.add).then_inc(s, 1)
                        own(f"cs{d}")
                        dve.tensor_tensor(exb, csb, sw, ALU.subtract).then_inc(s, 1)
                        dve.tensor_tensor(bd(tb), seq(None, c, d, emit), a, ALU.mult).then_inc(s, 1)
                        dve.scalar_tensor_tensor(bd(tk), a, -1.0, col("k_a", 0, 4).unsqueeze(2).to_broadcast([P, 4, L]),
                                                 ALU.add, ALU.mult).then_inc(s, 1)
                        own(f"ka{d}")
                        dve.scalar_tensor_tensor(bd(tk), bd(tk), 1.0, seq(4, c, d, emit), ALU.add, ALU.mult).then_inc(s, 1)
                        A(f"pv{d}")
                        E_(f"bT{d}", c - 1)
                        for r, k in H:
                            dve.tensor_tensor(g["bt"][r, :, k], bd(tb)[r], bd(pinv)[r], ALU.mult).then_inc(s, 1)
                        own(f"kd{d}")
                        for r, k in H:
                            dve.tensor_tensor(g["kt"][r, :, k], bd(tk)[r], bd(pinv)[r], ALU.mult).then_inc(s, 1)
                        dve.tensor_copy(plast[d], bd(pinc)[:, :, (L - 1) * (1 - d)]).then_inc(s, 1)
                    for d in range(2):
                        g, B = dirs[d], 4 * d
                        lo, up = (1, 7) if d == 0 else (7, 1)
                        E_(f"A{d}")
                        dve.tensor_tensor(g["Ym"], P4(B + 1), m4(lo), ALU.mult).then_inc(s, 1)
                        own(f"m{d}")
                        dve.tensor_tensor(g["X"], I4, g["Ym"], ALU.subtract).then_inc(s, 1)
                        A(f"AT{d}")
                        dve.tensor_tensor(g["XT"], g["AT"], m4(up), ALU.mult).then_inc(s, 1)
                        own(f"n{d}")
                        dve.tensor_tensor(g["XT"], I4, g["XT"], ALU.subtract).then_inc(s, 1)
                        E_(f"CT{d}")
                        dve.tensor_tensor(g["CT"], P4(B + 2), m4(14 - d), ALU.mult).then_inc(s, 1)
                        if emit:
                            E_(f"R1{d}")
                            dve.tensor_tensor(g["R1"], P4(B + 3), m4(16 - d), ALU.mult).then_inc(s, 1)
                            E_(f"R2{d}")
                            dve.tensor_tensor(g["R2"], P4(B), m4(16 - d), ALU.mult).then_inc(s, 1)
                    for l in LV:
                        for d in range(2):
                            g, B = dirs[d], 4 * d
                            E_(f"Y{l}{d}")
                            own(f"x{l - 1}{d}")
                            dve.tensor_tensor(g["Ym"], P4(B), m4((1 if d == 0 else 7) + l), ALU.mult).then_inc(s, 1)
                        for d in range(2):
                            g, B = dirs[d], 4 * d
                            if l < 5:
                                E_(f"XY{l}{d}")
                                dve.tensor_tensor(g["X"], g["X"], P4(B + 1), ALU.subtract).then_inc(s, 1)
                            E_(f"YX{l}{d}")
                            own(f"xt{l - 1}{d}")
                            dve.tensor_tensor(g["XT"], g["XT"], P4(B + 2), ALU.subtract).then_inc(s, 1)
                    for d in range(2):
                        E_(f"G{d}")
                        dve.tensor_copy(dirs[d]["G"], bd(psum[:, 4 * d + 3, 0:4 * L])).then_inc(s, 1)
                    for d in range(2):
                        g, B = dirs[d], 4 * d
                        E_(f"y{d}" if emit else f"Z{d}")
                        dve.tensor_tensor(g["st"], g["st"], bd(psum[:, B, 0:4 * L]), ALU.add).then_inc(s, 1)
                        own(f"z{d}")
                        dve.tensor_tensor(g["st"], g["st"], plast[d].unsqueeze(2).to_broadcast([P, 4, L]), ALU.mult).then_inc(s, 1)
                        if emit:
                            n = bass.ds(c, 1) if d == 0 else bass.ds(c * -1 + 7, 1)
                            own("zz0") if d == 0 else own("y0")
                            acc = yacc[:, n, :, :].rearrange("p c q v -> p (c q) v")
                            dve.tensor_tensor(acc, acc, bd(psum[:, B + 1, 0:4 * L]), ALU.add).then_inc(s, 1)
            rwkv_out_dve(dve)

        E0 = N0 + 4 * T
        bon = mem[:, E0:E0 + 4 * T].rearrange("p (q t) -> p q t", q=4)
        gat = mem[:, E0 + 4 * T:E0 + 8 * T].rearrange("p (q t) -> p q t", q=4)
        ybd = [bd(mem[:, 15 * TA + 2048 + n * 512:15 * TA + 2560 + n * 512]) for n in range(2)]
        gst = mem[:, 15 * TA + 3072:15 * TA + 3200].rearrange("p (s n) -> p s n", s=4)
        sgl = res_f[:, 0:T]
        rk3 = mem[:, 15 * TA + 3200:15 * TA + 3200 + 2 * T].rearrange("p (b t) -> p b t", b=2)
        xa = Steps(sem("rwkv_out_act"), "sgl sq std g0 g1 g2 g3 " + " ".join(f"c{c}" for c in range(8)))
        xd = Steps(sem("rwkv_out_dve"), "sum mu cen var " + " ".join(f"p{q} r{q} b{q}" for q in range(4)) + " is "
                   + " ".join(f"ya{c} yb{c}" for c in range(8)) + " f0 f1 f2 f3")
        xe = Steps(sem("rwkv_out_pe"), "g0 g1 g2 g3 b0 b1 b2 b3 " + " ".join(f"t{c}" for c in range(8)))
        xz = sem("ybd_zero")
        ye = Steps(sem("rwkv_ya"), "y")
        ysq = res_f[:, T:T + 2048].rearrange("p (n v) -> p n v", v=L)
        yrows = yacc.rearrange("p c q v -> p (c q) v")

        def rwkv_out_pe(pe):
            rd = RS[True][1]
            pe.wait_ge(rd.sem, rd.end(8))
            pe.wait_ge(xa.sem, xa.at(0, "sgl"))
            for q in range(4):
                pe.matmul(psum[:, q, :], wg[:, q // 2, q % 2 * P:(q % 2 + 1) * P], sgl,
                          start=True, stop=True).then_inc(xe.sem, 1)
            for q in range(4):
                pe.wait_ge(xd.sem, xd.at(0, f"r{q}"))
                pe.matmul(psum[:, 4 + q % 2, :], same_head, rk3[:, q % 2, :], start=True, stop=True).then_inc(xe.sem, 1)
            for c in range(8):
                pe.wait_ge(xd.sem, xd.at(0, f"yb{c}"))
                if c >= 2:
                    pe.wait_ge(xa.sem, xa.at(0, f"c{c - 2}"))
                for q in range(4):
                    ins = pe.matmul(psum[:, 6 + c % 2, q * L:(q + 1) * L], ybd[c % 2][:, q, :], two_ident, start=True, stop=True)
                ins.then_inc(xe.sem, 1)

        def rwkv_out_act(act):
            rd = RS[True][1]
            s = xa.sem
            act.wait_ge(rd.sem, rd.end(8))
            act.activation(sgl, Z[:, 14, 0:T], ACT.Sigmoid).then_inc(s, 1)
            act.wait_ge(xd.sem, xd.at(0, "cen"))
            act.activation(ysq, yrows, ACT.Square).then_inc(s, 1)
            act.wait_ge(xd.sem, xd.at(0, "var"))
            act.activation(gst[:, 2, :], gst[:, 1, :], ACT.Sqrt, bias=eps[:, 4:5], scale=1.0 / L).then_inc(s, 1)
            for q in range(4):
                act.wait_ge(xe.sem, xe.at(0, f"g{q}"))
                act.activation(gat[:, q, :], psum[:, q, :], ACT.Copy).then_inc(s, 1)
            for c in range(8):
                act.wait_ge(xe.sem, xe.at(0, f"t{c}"))
                act.activation(ya[:, :, c * L:(c + 1) * L], bd(psum[:, 6 + c % 2, 0:4 * L]), ACT.Copy).then_inc(s, 1)

        def rwkv_out_dve(dve):
            s = xd.sem
            own = lambda n: dve.wait_ge(s, xd.at(0, n))
            rd = RS[True][1]
            dve.wait_ge(rd.sem, rd.end(8))
            dve.tensor_reduce(gst[:, 0, :], yrows, AX.X, ALU.add).then_inc(s, 1)
            own("sum")
            dve.tensor_scalar(gst[:, 0, :], gst[:, 0, :], 1.0 / L, None, ALU.mult).then_inc(s, 1)
            own("mu")
            dve.tensor_tensor(yrows, yrows, gst[:, 0, :].unsqueeze(2).to_broadcast([P, 32, L]), ALU.subtract).then_inc(s, 1)
            dve.wait_ge(xa.sem, xa.at(0, "sq"))
            dve.tensor_reduce(gst[:, 1, :], ysq, AX.X, ALU.add).then_inc(s, 1)
            for q in range(4):
                if q >= 2:
                    dve.wait_ge(xe.sem, xe.at(0, f"b{q - 2}"))
                dve.tensor_tensor(rk3[:, q % 2, :], Z[:, q, 0:T], Z[:, 4 + q, 0:T], ALU.mult).then_inc(s, 1)
                own(f"p{q}")
                dve.tensor_scalar(rk3[:, q % 2, :], rk3[:, q % 2, :], col("r_k", q), None, ALU.mult).then_inc(s, 1)
                dve.wait_ge(xe.sem, xe.at(0, f"b{q}"))
                dve.tensor_tensor(bon[:, q, :], psum[:, 4 + q % 2, :], Z[:, 8 + q, 0:T], ALU.mult).then_inc(s, 1)
            dve.wait_ge(xa.sem, xa.at(0, "std"))
            dve.reciprocal(gst[:, 3, :], gst[:, 2, :]).then_inc(s, 1)
            own("is")
            dve.wait_ge(xz, 2)
            for c in range(8):
                if c >= 2:
                    dve.wait_ge(xe.sem, xe.at(0, f"t{c - 2}"))
                for h in range(2):
                    r = slice(64 * h, 64 * h + 64)
                    dve.tensor_tensor(ybd[c % 2][r, :, r], yacc[r, c, :, :], gst[r, 3, 4 * c:4 * c + 4].unsqueeze(2).to_broadcast([64, 4, L]),
                                      ALU.mult).then_inc(s, 1)
            dve.wait_ge(xa.sem, xa.at(0, "c7"))
            for q in range(4):
                dve.scalar_tensor_tensor(ya[:, q, :], ya[:, q, :], col("ln_g", q), bon[:, q, :], ALU.mult, ALU.add).then_inc(s, 1)
            for q in range(4):
                own(f"f{q}")
                dve.scalar_tensor_tensor(ya[:, q, :], ya[:, q, :], col("ln_b", q), gat[:, q, :], ALU.add, ALU.mult).then_inc(ye.sem, 1)

        def rwkv_out_pool(pool):
            re = RS[True][3]
            pool.wait_ge(re.sem, re.end(8))
            rd = RS[True][1]
            pool.wait_ge(rd.sem, rd.end(8))
            for n in range(2):
                pool.memset(ybd[n], 0.0).then_inc(xz, 1)

        merged2 = mem[:, 0:DT * T].rearrange("p (m t) -> p m t", t=T)
        gs = mem[:, DT * T:DT * T + 4 * T].rearrange("p (b s t) -> p b s t", b=2, s=2)
        m2a = Steps(sem("merge2_act"), "ga gb")
        m2d = Steps(sem("merge2_dve"), "a b s")
        m2a.base, m2d.base = 2 * 2, 2 * 3
        reloaded = sem("reloaded")

        def merge2_pool(pool):
            pool.wait_ge(ye.sem, 4)
            pool.dma_start(resid[:, :, :], spill).then_inc(reloaded, 16)

        def merge2_pe(pe):
            pe.wait_ge(ye.sem, 4)
            with pe.Fori(0, 2) as i:
                for mm in range(4):
                    bank = 4 * (mm % 2)
                    pe.wait_ge(m2d.sem, m2d.at(4 * i + (mm - 2), "b"))
                    for g in range(2):
                        w = use_slab(pe, "merge2", 3 * mm + g, i, 12)
                        for k in range(DT):
                            ins = pe.matmul(psum[:, bank + g, :], w[:, k, :], xn[:, k, :], start=k == 0, stop=k == DT - 1)
                        ins.then_inc(slab_used, 1)
                    w = use_slab(pe, "merge2", 3 * mm + 2, i, 12)
                    for b, y in ((0, ya), (1, yb)):
                        for k in range(4):
                            ins = pe.matmul(psum[:, bank + 2 + b, :], w[:, 4 * b + k, :], y[:, k, :], start=k == 0, stop=k == 3)
                    ins.then_inc(slab_used, 1)
            pe.wait_ge(m2d.sem, m2d.end(8))
            with pe.Fori(0, 2) as i:
                for mm in range(4):
                    w = use_slab(pe, "out2", mm, i, 4)
                    for k in range(DT):
                        ins = pe.matmul(psum[:, bass.ds(4 * i + mm, 1), :].rearrange("p a t -> p (a t)"), w[:, k, :], merged2[:, k, :],
                                        start=k == 0, stop=k == DT - 1)
                    ins.then_inc(slab_used, 1)

        def merge2_act(act):
            act.wait_ge(ye.sem, 4)
            act.sem_inc(m2a.sem, m2a.base)
            with act.Fori(0, 4) as i:
                for mm in range(2):
                    act.wait_ge(m2d.sem, m2d.at(2 * i + (mm - 2), "s"))
                    for g in range(2):
                        act.wait_ge(slab_used, 6 * i + (SLAB_AT["merge2"] + 3 * mm + g + 1))
                        act.activation(gs[:, mm, g, :], psum[:, 4 * mm + g, :], ACT.Sigmoid).then_inc(m2a.sem, 1)

        def merge2_dve(dve):
            s = m2d.sem
            dve.sem_inc(s, m2d.base)
            with dve.Fori(0, 4) as i:
                for mm in range(2):
                    dve.wait_ge(slab_used, 6 * i + (SLAB_AT["merge2"] + 3 * mm + 3))
                    for g, name in enumerate(("ga", "gb")):
                        dve.wait_ge(m2a.sem, m2a.at(2 * i + mm, name))
                        dve.tensor_tensor(gs[:, mm, g, :], gs[:, mm, g, :], psum[:, 4 * mm + 2 + g, :], ALU.mult).then_inc(s, 1)
                    dve.wait_ge(s, m2d.at(2 * i + mm, "b"))
                    dve.tensor_tensor(merged2[:, bass.ds(2 * i + mm, 1), :].rearrange("p a t -> p (a t)"), gs[:, mm, 0, :], gs[:, mm, 1, :],
                                      ALU.add).then_inc(s, 1)
            dve.wait_ge(reloaded, 16)
            for m in range(DT):
                dve.wait_ge(slab_used, SLAB_AT["out2"] + m + 1)
                dve.scalar_tensor_tensor(resid[:, m, :], psum[:, m, :], modv[:, 2 * DT + m, 0:1], resid[:, m, :],
                                         ALU.mult, ALU.add).then_inc(resid_ready, 1)

        R0 = 13568
        hid2 = part_of_mem("hid2_hi", R0, [4, T])
        mgu = mem[:, R0 + 4 * T:R0 + 6 * T].rearrange("p (b t) -> p b t", t=T)
        hid2_lo = part_of_mem("hid2_lo", R0 + 6 * T, [4, T])
        moe_xh = part_of_mem("moe_xh", 0, [DT, T])
        acc2 = mem[:, 6144:6144 + DT * T].rearrange("p (m t) -> p m t", t=T)
        ra_ = mem[:, 10240:10240 + 1280]
        rw = ra_[:, 0:160]
        rt = [ra_[:, 160 + 64 * n:224 + 64 * n] for n in range(10)]
        gate_t = mem[0:16, 11520:12032]
        gb = mem[:, R0 + 10 * T:R0 + 26 * T].rearrange("p (e t) -> p e t", t=T)
        router_in = sem("router_in")
        router_pe = sem("router_pe")
        router_act = sem("router_act")
        acc_zero = sem("acc_zero")
        gates_out = sem("gates_out")
        gate_in = sem("gate_in")
        out_ready = sem("out_ready")
        stored = sem("stored")
        rs = Steps(sem("router_dve"), "lg den score sel hi lo top mid lo1 sec grp best eqg pick mxg ing pen mul msel "
                   + " cut ".join(f"mx{n} eq{n} w{n} pk{n} oh{n}" for n in range(2)) + " chosen cs sum inv gate")
        moe_sig = sem("moe_sig")
        moe_hi = sem("moe_hi")
        moe_d = Steps(sem("moe_dve"), " ".join(f"s{j} g{j} r{j} h{j}" for j in range(4)) + " " + " ".join(f"c{m}" for m in range(DT)))
        moe_d.base = len(moe_d.names)

        def moe_pool(pool):
            pool.wait_ge(ye.sem, 4)
            pool.dma_start(rw, router_w).then_inc(router_in, 16)
            pool.memset(acc2, 0.0).then_inc(acc_zero, 1)
            pool.wait_ge(router_act, 2)
            pool.wait_ge(m2d.sem, m2d.end(8))
            pool.dma_start(gates_dram, gate_t).then_inc(gates_out, 16)
            pool.wait_ge(gates_out, 16)
            with pool.Fori(0, 12 * E // 4) as i:
                for j in range(4):
                    split_lo(pool, "moe", j, i, 4)
            for m in range(0, DT, 2):
                pool.wait_ge(out_ready, m + 2)
                pool.dma_start(out[:, m:m + 2, :], resid[:, m:m + 2, :]).then_inc(stored, 16)
            pool.wait_ge(spilled, 16)
            pool.wait_ge(stored, 64)

        def moe_pe(pe):
            norm_pe(pe, 5)
            pe.wait_ge(xn_ready, 6 * DT)
            pe.wait_ge(router_in, 16)
            for t in range(4):
                for k in range(DT):
                    ins = pe.matmul(psum[:, 0, t * E:(t + 1) * E], xn[:, k, t * P:(t + 1) * P], rw[:, k * E:(k + 1) * E],
                                    start=k == 0, stop=k == DT - 1)
            ins.then_inc(router_pe, 1)
            pe.wait_ge(rs.sem, rs.at(0, "gate"))
            for t in range(4):
                ins = pe.transpose(psum[0:16, 1, t * P:(t + 1) * P], rt[9][:, t * E:(t + 1) * E], ident[:, :])
            ins.then_inc(router_pe, 1)
            pe.wait_ge(router_act, 2)
            pe.wait_ge(x_lo, 3 * DT)
            with pe.Fori(0, E) as e:
                for j in range(4):
                    b = 2 * (j % 2)
                    pe.wait_ge(moe_d.sem, moe_d.at(e, f"g{j - 2}") if j >= 2 else moe_d.at(e - 1, f"g{j + 2}"))
                    for n in range(2):
                        w = use_split(pe, "moe", 2 * j + n, e, 12)
                        for k in range(DT):
                            ins = product(pe, psum[:, b + n, :], w, k, moe_xh[:, k, :], xn_r[:, k, :], k == 0, k == DT - 1)
                        ins.then_inc(slab_used, 1)
                for n in range(4):
                    w = use_split(pe, "moe", 8 + n, e, 12)
                    for mm, k in [(0, 0), (0, 1), (0, 2), (1, 0), (1, 1), (1, 2), (0, 3), (1, 3)]:
                        m = 2 * n + mm
                        if k == 0:
                            pe.wait_ge(moe_d.sem, moe_d.at(e, f"c{m - 4}") if m >= 4 else moe_d.at(e - 1, f"c{m + 4}"))
                        if n == 0 and mm == 0:
                            pe.wait_ge(moe_d.sem, moe_d.at(e, f"h{k}"))
                        ins = product(pe, psum[:, 4 + m % 4, :], w, 4 * mm + k, hid2[:, k, :], hid2_lo[:, k, :], k == 0, k == 3)
                    ins.then_inc(slab_used, 1)

        def moe_act(act):
            norm_act(act, 5, 4 * DT)
            split_hi(act, "moe", 0)
            split_hi(act, "moe", 1)
            x_hi_act(act, 2, 5, moe_xh)
            act.wait_ge(rs.sem, rs.at(0, "lg"))
            act.activation(rt[0], rt[0], ACT.Exp, scale=-1.0).then_inc(router_act, 1)
            act.wait_ge(router_pe, 2)
            act.activation(gate_t, psum[0:16, 1, :], ACT.Copy).then_inc(router_act, 1)
            act.wait_ge(gates_out, 16)
            act.sem_inc(gate_in, 16)

            def expert(e, last):
                act.wait_ge(gate_in, e * 16 + 16)
                act.dma_start(gb[:, bass.ds(e, 1), :], gates_dram[bass.ds(e, 1), :].partition_broadcast(P)).then_inc(gate_in, 16)
                for j in range(4):
                    split_hi(act, "moe", 2 * j + 2, e, 12)
                    split_hi(act, "moe", 2 * j + 3, e, 12)
                    act.wait_ge(moe_d.sem, moe_d.at(e, f"h{j - 2}") if j >= 2 else moe_d.at(e - 1, f"h{j + 2}"))
                    act.wait_ge(slab_used, e * 12 + (SLAB_AT["moe"] + 2 * j + 1))
                    act.activation(mgu[:, j % 2, :], psum[:, 2 * (j % 2), :], ACT.Sigmoid).then_inc(moe_sig, 1)
                    act.wait_ge(moe_d.sem, moe_d.at(e, f"r{j}"))
                    act.activation(hid2[:, j, :], mgu[:, j % 2, :], ACT.Copy).then_inc(moe_hi, 1)
                for n in (10, 11) if last else (10, 11, 12, 13):
                    split_hi(act, "moe", n, e, 12)

            with act.Fori(0, E - 1) as e:
                expert(e, False)
            expert(E - 1, True)

        def router_dve(dve):
            s = rs.sem
            own = lambda n: dve.wait_ge(s, rs.at(0, n))
            g4 = lambda v: v.rearrange("p (n e) -> p n e", e=4)
            g16 = lambda v: v.rearrange("p (n e) -> p n e", e=E)
            score, sel = rt[0], rt[1]
            small = lambda n, a, b: rt[n][:, a:b]
            hi2, lo2 = small(2, 0, 32).rearrange("p (n e) -> p n e", e=2), small(2, 32, 64).rearrange("p (n e) -> p n e", e=2)
            top, midd, sec, grp = (small(3, 16 * n, 16 * n + 16) for n in range(4))
            best, mxg = small(4, 0, 4), small(4, 4, 8)
            eqg = small(4, 16, 32)
            den, inv = small(4, 8, 12), small(4, 12, 16)
            ing = small(4, 32, 48)
            msel, pen = rt[5], rt[6]
            oh = [rt[7], rt[8]]
            gate = rt[9]
            desc = rw[:, 144:160]
            T_ = lambda name, need, *a: (own(need) if need else None, dve.tensor_tensor(*a).then_inc(s, 1))
            dve.wait_ge(router_in, 16)
            dve.wait_ge(router_pe, 1)
            dve.tensor_scalar(score, psum[:, 0, 0:64], -88.0, None, ALU.max).then_inc(s, 1)
            dve.wait_ge(router_act, 1)
            dve.tensor_scalar(score, score, 1.0, None, ALU.add).then_inc(s, 1)
            own("den")
            dve.reciprocal(score, score).then_inc(s, 1)
            T_("sel", "score", g16(sel), g16(score), rw[:, 128:144].unsqueeze(1).to_broadcast([P, 4, E]), ALU.add)
            T_("hi", "sel", hi2, g4(sel)[:, :, 0::2], g4(sel)[:, :, 1::2], ALU.max)
            T_("lo", None, lo2, g4(sel)[:, :, 0::2], g4(sel)[:, :, 1::2], ALU.min)
            T_("top", "lo", top, hi2[:, :, 0], hi2[:, :, 1], ALU.max)
            T_("mid", None, midd, hi2[:, :, 0], hi2[:, :, 1], ALU.min)
            T_("lo1", None, sec, lo2[:, :, 0], lo2[:, :, 1], ALU.max)
            T_("sec", "lo1", sec, midd, sec, ALU.max)
            T_("grp", "sec", grp, top, sec, ALU.add)
            own("grp")
            dve.tensor_reduce(best, g4(grp), AX.X, ALU.max).then_inc(s, 1)
            T_("eqg", "best", g4(eqg), g4(grp), best.unsqueeze(2).to_broadcast([P, 4, 4]), ALU.is_ge)
            T_("pick", "eqg", g4(eqg), g4(eqg), desc[:, 0:4].unsqueeze(1).to_broadcast([P, 4, 4]), ALU.mult)
            own("pick")
            dve.tensor_reduce(mxg, g4(eqg), AX.X, ALU.max).then_inc(s, 1)
            T_("ing", "mxg", g4(ing), g4(eqg), mxg.unsqueeze(2).to_broadcast([P, 4, 4]), ALU.is_ge)
            own("ing")
            dve.tensor_scalar(g4(pen), ing.unsqueeze(2).to_broadcast([P, 16, 4]), -1.0, 3.0e38, ALU.add, ALU.mult).then_inc(s, 1)
            T_("mul", None, g4(msel), g4(sel), ing.unsqueeze(2).to_broadcast([P, 16, 4]), ALU.mult)
            T_("msel", "mul", msel, msel, pen, ALU.add)
            for n in range(2):
                own("cut" if n else "msel")
                dve.tensor_reduce(best, g16(msel), AX.X, ALU.max).then_inc(s, 1)
                T_(f"eq{n}", f"mx{n}", g16(oh[n]), g16(msel), best.unsqueeze(2).to_broadcast([P, 4, E]), ALU.is_ge)
                T_("w", f"eq{n}", g16(oh[n]), g16(oh[n]), desc.unsqueeze(1).to_broadcast([P, 4, E]), ALU.mult)
                own(f"w{n}")
                dve.tensor_reduce(mxg, g16(oh[n]), AX.X, ALU.max).then_inc(s, 1)
                T_("oh", f"pk{n}", g16(oh[n]), g16(oh[n]), mxg.unsqueeze(2).to_broadcast([P, 4, E]), ALU.is_ge)
                if n == 0:
                    own("oh0")
                    dve.scalar_tensor_tensor(msel, oh[0], -3.0e38, msel, ALU.mult, ALU.add).then_inc(s, 1)
            T_("chosen", "oh1", oh[0], oh[0], oh[1], ALU.add)
            T_("cs", "chosen", gate, oh[0], score, ALU.mult)
            own("cs")
            dve.tensor_reduce(den, g16(gate), AX.X, ALU.add).then_inc(s, 1)
            own("sum")
            dve.reciprocal(inv, den).then_inc(s, 1)
            T_("gate", "inv", g16(gate), g16(gate), inv.unsqueeze(2).to_broadcast([P, 4, E]), ALU.mult)

        def moe_dve(dve):
            mod_norm_dve(dve, 5, lambda j: gm2[:, j:j + 1], lambda j: modv[:, 3 * DT + j, 0:1])
            router_dve(dve)
            x_lo_dve(dve, 2, moe_xh)
            s = moe_d.sem
            dve.sem_inc(s, moe_d.base)
            dve.wait_ge(acc_zero, 1)
            with dve.Fori(0, E) as e:
                own = lambda n: dve.wait_ge(s, moe_d.at(e, n))
                for j in range(4):
                    b, g = 2 * (j % 2), mgu[:, j % 2, :]
                    dve.wait_ge(moe_sig, e * 4 + (j + 1))
                    dve.tensor_tensor(g, g, psum[:, b, :], ALU.mult).then_inc(s, 1)
                    own(f"s{j}")
                    dve.wait_ge(slab_used, e * 12 + (SLAB_AT["moe"] + 2 * j + 2))
                    dve.tensor_tensor(g, g, psum[:, b + 1, :], ALU.mult).then_inc(s, 1)
                    own(f"g{j}")
                    dve.wait_ge(gate_in, e * 16 + 32)
                    dve.tensor_tensor(g, g, gb[:, bass.ds(e, 1), :].rearrange("p a t -> p (a t)"), ALU.mult).then_inc(s, 1)
                    dve.wait_ge(moe_hi, e * 4 + (j + 1))
                    dve.tensor_tensor(hid2_lo[:, j, :], g, f(hid2[:, j, :]), ALU.subtract).then_inc(s, 1)
                for m in range(DT):
                    dve.wait_ge(slab_used, e * 12 + (SLAB_AT["moe"] + 9 + m // 2))
                    dve.tensor_tensor(acc2[:, m, :], acc2[:, m, :], psum[:, 4 + m % 4, :], ALU.add).then_inc(s, 1)
            for m in range(DT):
                dve.wait_ge(s, moe_d.at(E - 1, f"c{m}"))
                dve.scalar_tensor_tensor(resid[:, m, :], acc2[:, m, :], modv[:, 5 * DT + m, 0:1], resid[:, m, :],
                                         ALU.mult, ALU.add).then_inc(out_ready, 1)

        block = ctx.enter_context(nc.Block())

        @block.sync
        def _(sp):
            start_sync(sp)
            stream_sync(sp)

        @block.gpsimd
        def _(pool):
            start_pool(pool)
            ffn_pool(pool, 0)
            hgrn_pool(pool)
            lru_pool(pool)
            ffn_pool(pool, 1)
            block2_pool(pool)

        @block.scalar
        def _(act):
            start_act(act)
            act.activation(cs[:, :], col("c", 0, 2 * DT), ACT.Sigmoid).then_inc(cs_act, 1)
            norm_act(act, 0, 0)
            ffn_act(act, 0)
            norm_act(act, 1, 8)
            hgrn_act(act)
            lru_act(act)
            merge_act(act)
            norm_act(act, 2, 16)
            ffn_act(act, 1)
            norm_act(act, 3, 24)
            block2_act(act)

        @block.tensor
        def _(pe):
            norm_pe(pe, 0)
            ffn_pe(pe, 0)
            norm_pe(pe, 1)
            hgrn_pe(pe)
            lru_pe(pe)
            merge_pe(pe)
            norm_pe(pe, 2)
            ffn_pe(pe, 1)
            mod_pe(pe)
            norm_pe(pe, 3)
            block2_pe(pe)

        @block.vector
        def _(dve):
            dve.sem_inc(hid_ready, 2)
            start_dve(dve)
            dve.wait_ge(cs_act, 1)
            dve.tensor_tensor(cs[:, :], cs[:, :], col("c", 0, 2 * DT), ALU.mult).then_inc(cs_dve, 1)
            norm_dve(dve, 0, "norm_ffn1", xn)
            ffn_dve(dve, 0)
            norm_dve(dve, 1, "norm_mix", xn)
            hgrn_dve(dve)
            lru_dve(dve)
            merge_dve(dve)
            norm_dve(dve, 2, "norm_ffn2", xn)
            ffn_dve(dve, 1)
            norm_dve(dve, 3, "norm_final", resid)
            block2_dve(dve)


def columns(v):
    v = np.asarray(v)
    return v.reshape(-1, P).T


def k_slabs(w):
    w = np.asarray(w)
    m = w.shape[1] // P
    return w.reshape(DT, P, m, P).transpose(2, 1, 0, 3)


def constants():
    a, b = np.arange(P)[:, None], np.arange(P)[None, :]
    same_head = (a // 64 == b // 64)
    t, s = a % 64, b % 64
    out = [same_head]
    low = []
    for L in (1, 2, 4, 8, 16, 32):
        low.append(same_head & (t // (2 * L) == s // (2 * L)) & (t // L % 2 == 1) & (s // L % 2 == 0))
    out += low + [m.T for m in low]
    out += [same_head & (s < t), same_head & (s > t), same_head & (s <= t), same_head & (s >= t)]
    out += [np.concatenate([np.eye(64), np.eye(64)])]
    q, k = a % 64, np.arange(64)[None, :]
    first = np.clip(q - 8, 0, 48)
    out += [np.where((k >= first) & (k < first + 16), 0.0, -3.0e38)]
    return np.concatenate([m.astype(np.float32) for m in out], axis=1)


def bias_rows(rpb):
    h = rpb.shape[0]
    padded = np.zeros((h, 17, 127), np.float32)
    padded[:, 1:16, 48:79] = rpb
    q, k = np.arange(64)[:, None], np.arange(64)[None, :]
    rows = padded[:, :, k - q + 63]
    two = np.stack([rows[:, 1:17], rows[:, 0:16]], axis=1)
    return two.transpose(0, 1, 3, 2, 4).reshape(h, P, 1024)


def lora_rows(i):
    w = i["rw_w_lora_b_2"][0].reshape(P, 512)
    a = i["rw_a_lora_b_2"][0].reshape(P, 512)
    return np.stack([w, a, i["rw_g_lora_b_2"][0]], axis=1)


def router_rows(i):
    w = i["router_w_2"].reshape(DT, P, E).transpose(1, 0, 2).reshape(P, DT * E)
    bias = np.broadcast_to(i["router_bias_2"], (P, E))
    order = np.broadcast_to(np.arange(E, 0, -1, dtype=np.float32), (P, E))
    return np.concatenate([w, bias, order], axis=1)


def lay_out(inputs):
    i = {k: np.asarray(v) for k, v in inputs.items()}
    parts = []

    def ffn(w_in, w_out):
        s = k_slabs(w_in)
        parts.append(s.reshape(2, FT, P, SLAB, P).transpose(1, 0, 2, 3, 4).reshape(2 * FT, P, SLAB, P))
        parts.append(w_out.reshape(FT, P, SLAB, P))

    ffn(i["ffn1_w_in"][0], i["ffn1_w_out"][0])
    mix = k_slabs(i["w_in_mix"][0]).reshape(11, DT, P, SLAB, P)
    parts.append(mix[[0, 3, 1, 2]].transpose(1, 0, 2, 3, 4).reshape(-1, P, SLAB, P))
    parts.append(mix[[4, 5, 6, 7]].transpose(1, 0, 2, 3, 4).reshape(-1, P, SLAB, P))
    branch = np.stack([k_slabs(i["w_branch"][0, b]) for b in range(3)])
    parts.append(np.concatenate([mix[8:11], branch]).transpose(1, 0, 2, 3, 4).reshape(-1, P, SLAB, P))
    parts.append(k_slabs(i["w_out_mix"][0]))
    ffn(i["ffn2_w_in"][0], i["ffn2_w_out"][0])
    parts.append(k_slabs(i["mod_w_2"][0]))
    in2 = i["w_in_2"][0]
    parts.append(k_slabs(in2[:, 0:2944]))
    parts.append(in2[:, 2944:3456].reshape(4, 2, P, 4, P).transpose(0, 2, 1, 3, 4).reshape(4, P, SLAB, P))
    gates = k_slabs(in2[:, 3456:5504]).reshape(2, DT, P, SLAB, P)
    proj = np.concatenate([i["proj_a_2"][0], i["proj_b_2"][0]])
    parts.append(np.concatenate([gates, k_slabs(proj)[None]]).transpose(1, 0, 2, 3, 4).reshape(-1, P, SLAB, P))
    parts.append(k_slabs(i["w_out_2"][0]))
    for e in range(E):
        w13 = np.stack([k_slabs(i["moe_w1_2"][0, e]), k_slabs(i["moe_w3_2"][0, e])])
        parts.append(w13.transpose(1, 0, 2, 3, 4).reshape(8, P, SLAB, P))
        w2 = i["moe_w2_2"][0, e].reshape(4, P, 4, 2, P).transpose(2, 1, 3, 0, 4)
        parts.append(w2.reshape(4, P, SLAB, P))
    stream = np.concatenate(parts)
    assert stream.shape[0] == N_SLABS, (stream.shape, N_SLABS)

    two = lambda v: np.concatenate([v, v])
    table = {
        "norm_ffn1": i["norm_ffn1"], "norm_mix": i["norm_mix"], "norm_ffn2": i["norm_ffn2"],
        "norm_final": i["norm_final"], "norm1": i["norm1_g_2"], "norm2": i["norm2_g_2"], "b_mix": i["b_in_mix"],
        "lb_logits": i["hgrn_lb_logits"], "hg_norm": i["hg_norm"], "lru_conv_w": i["lru_conv_w"],
        "lru_conv_b": i["lru_conv_b"], "gate_b": i["lru_gate_b"], "lambda": i["lru_lambda"], "cv_w": i["cv_dw_w"],
        "cv_b": i["cv_dw_b"], "cv_ln_g": i["cv_ln_g"], "cv_ln_b": i["cv_ln_b"], "mod_b": i["mod_b_2"],
        "w0": i["rw_w0_2"], "a0": i["rw_a0_2"], "k_k": i["rw_k_k_2"], "k_a": i["rw_k_a_2"], "r_k": i["rw_r_k_2"],
        "ln_g": i["rw_ln_g_2"], "ln_b": i["rw_ln_b_2"], "q_g": two(i["na_q_g_2"][0]), "k_g": two(i["na_k_g_2"][0]),
        "c": np.stack([i["c_2"][0], i["c_ctx_2"]]),
    }
    cols = []
    for name, n in PAR:
        c = columns(table[name])
        assert c.shape == (P, n), name
        cols.append(c)
    return {
        "stream": stream,
        "par": np.concatenate(cols, axis=1),
        "x_t": i["x"][0].T.reshape(DT, P, T).transpose(1, 0, 2),
        "vbias": i["b_in_mix"][0, 2048:3072].reshape(1, D),
        "gate_w": i["lru_gate_w"][0].transpose(2, 1, 0, 3),
        "masks": constants(),
        "ctx_t": i["ctx_2"][0].T.reshape(DT, P, TC).transpose(1, 0, 2),
        "rpb": bias_rows(i["na_rpb_2"][0]),
        "router_w": router_rows(i),
        "lora": lora_rows(i),
    }


def kernel(**inputs):
    import concourse.bacc as bacc
    from concourse.bass_utils import run_bass_kernel_spmd

    arrays = {name: np.ascontiguousarray(a) for name, a in lay_out(inputs).items()}
    nc = bacc.Bacc("TRN2", target_bir_lowering=False, num_devices=1)
    args = {name: nc.dram_tensor(name, list(a.shape), F32, kind="ExternalInput").ap() for name, a in arrays.items()}
    args["spill"] = nc.dram_tensor("spill", [P, DT, T], F32).ap()
    args["gates_dram"] = nc.dram_tensor("gates_dram", [E, T], F32).ap()
    args["out"] = nc.dram_tensor("out", [P, DT, T], F32, kind="ExternalOutput").ap()
    hybrid_block_kernel(nc, **args)
    r = run_bass_kernel_spmd(nc, [arrays], core_ids=[0])
    got = np.asarray(r.results[0]["out"])
    return got.transpose(2, 1, 0).reshape(1, T, D)
```
